# Optimizing a Trainium2 kernel written in Bass

```python
import math
import jax, jax.numpy as jnp
from jax import lax
import numpy as np

D_MODEL = 1024
BATCH = 1
SEQ = 1024
DEPTH = 1
DEC_BATCH = 8
DEC_SEQ = 8
PAST_LEN = 1024
PAGE_SIZE = 128

DIL_GROUPS = ((128, 1), (512, 4), (2048, 16))
N_GROUPS = 3
N_SLOTS = 8
HEAD_DIM = 64
ATT_W = N_GROUPS * N_SLOTS * HEAD_DIM
ATT_OUT = N_SLOTS * HEAD_DIM
ROPE_THETA = 10000.0
BAND_BLOCK = 128
D_CONV = D_MODEL
CONV_WIDTH = 3
PEER_HEADS = 8
PEER_N_KEYS = 128
PEER_N_EXPERTS = PEER_N_KEYS * PEER_N_KEYS
PEER_D_KEY = 256
PEER_TOPK = 16
PEER_CHUNK = 128
LN_EPS = 1e-5
DEEPNORM_ALPHA = (2.0 * DEPTH) ** 0.25
DEEPNORM_BETA = (8.0 * DEPTH) ** -0.25
N_IN = 3 * ATT_W + 3 * D_CONV + 2 * D_MODEL
NEG_INF = -1e30

kernel_name = "dilated_conv_peer_hybrid_step"

def layer_norm(x, g, b):
    xf = x.astype(jnp.float32)
    mu = jnp.mean(xf, axis=-1, keepdims=True)
    var = jnp.mean(jnp.square(xf - mu), axis=-1, keepdims=True)
    y = (xf - mu) * lax.rsqrt(var + LN_EPS) * g.astype(jnp.float32) + b.astype(jnp.float32)
    return y.astype(x.dtype)

def rope(x, pos):
    half = HEAD_DIM // 2
    inv_freq = ROPE_THETA ** (-jnp.arange(half, dtype=jnp.float32) / half)
    ang = pos.astype(jnp.float32)[:, None] * inv_freq[None, :]
    cos = jnp.cos(ang)[:, None, None, :]
    sin = jnp.sin(ang)[:, None, None, :]
    xf = x.astype(jnp.float32)
    x1, x2 = xf[..., :half], xf[..., half:]
    return jnp.concatenate([x1 * cos - x2 * sin, x2 * cos + x1 * sin], axis=-1).astype(x.dtype)

def mixer_projections(x, pos, w_in):
    n, s, _ = x.shape
    z = jnp.einsum('nsd,de->nse', x, w_in)
    bounds = [ATT_W, 2 * ATT_W, 3 * ATT_W, 3 * ATT_W + D_CONV, 3 * ATT_W + 2 * D_CONV,
              3 * ATT_W + 3 * D_CONV, 3 * ATT_W + 3 * D_CONV + D_MODEL]
    q, k, v, c_in, c_b, c_c, g_a, g_c = jnp.split(z, bounds, axis=-1)
    q = rope(q.reshape(n, s, N_GROUPS, N_SLOTS, HEAD_DIM), pos)
    k = rope(k.reshape(n, s, N_GROUPS, N_SLOTS, HEAD_DIM), pos)
    v = v.reshape(n, s, N_GROUPS, N_SLOTS, HEAD_DIM)
    u = c_c * c_in
    return q, k, v, u, c_b, g_a, g_c

def dilated_band_attention(q, k, v, dil, span):
    n, s, h, c = q.shape
    m = s // dil
    nb = -(-m // BAND_BLOCK)
    mp = nb * BAND_BLOCK

    def to_blocks(a):
        a = a.reshape(n, m, dil, h, c).transpose(0, 2, 1, 3, 4)
        a = jnp.pad(a, ((0, 0), (0, 0), (0, mp - m), (0, 0), (0, 0)))
        return a.reshape(n, dil, nb, BAND_BLOCK, h, c).astype(jnp.float32)

    qb, kb, vb = to_blocks(q), to_blocks(k), to_blocks(v)

    def with_prev(a):
        prev = jnp.pad(a, ((0, 0), (0, 0), (1, 0), (0, 0), (0, 0), (0, 0)))[:, :, :nb]
        return jnp.concatenate([prev, a], axis=3)

    kk, vv = with_prev(kb), with_prev(vb)
    scores = jnp.einsum('brnqhc,brnkhc->brnhqk', qb, kk) * (c ** -0.5)
    qi = jnp.arange(BAND_BLOCK)[:, None]
    ki = jnp.arange(2 * BAND_BLOCK)[None, :]
    dist = BAND_BLOCK + qi - ki
    in_band = (dist >= 0) & (dist <= span)
    has_prev = (jnp.arange(nb) > 0)[:, None, None] | (ki >= BAND_BLOCK)[None]
    mask = in_band[None] & has_prev
    scores = jnp.where(mask[:, None], scores, NEG_INF)
    mx = jnp.max(scores, axis=-1, keepdims=True)
    p = jnp.exp(scores - mx)
    den = jnp.sum(p, axis=-1, keepdims=True)
    out = jnp.einsum('brnhqk,brnkhc->brnqhc', p / den, vv)
    lse = (mx + jnp.log(den))[..., 0]
    out = out.reshape(n, dil, mp, h, c)[:, :, :m].transpose(0, 2, 1, 3, 4).reshape(n, s, h, c)
    lse = lse.transpose(0, 1, 2, 4, 3).reshape(n, dil, mp, h)[:, :, :m].transpose(0, 2, 1, 3).reshape(n, s, h)
    return out, lse

def dilated_cached_attention(q, k_all, v_all, n_prev, dil, span):
    t = q.shape[1]
    c = q.shape[-1]
    idx = n_prev + jnp.arange(t)[:, None] - dil * jnp.arange(span + 1)[None, :]
    valid = idx >= 0
    idx = jnp.maximum(idx, 0)
    kg = jnp.take(k_all, idx, axis=1).astype(jnp.float32)
    vg = jnp.take(v_all, idx, axis=1).astype(jnp.float32)
    scores = jnp.einsum('nthc,ntjhc->nthj', q.astype(jnp.float32), kg) * (c ** -0.5)
    scores = jnp.where(valid[None, :, None, :], scores, NEG_INF)
    mx = jnp.max(scores, axis=-1, keepdims=True)
    p = jnp.exp(scores - mx)
    den = jnp.sum(p, axis=-1, keepdims=True)
    out = jnp.einsum('nthj,ntjhc->nthc', p / den, vg)
    lse = (mx + jnp.log(den))[..., 0]
    return out, lse

def combine_groups(outs, lses, dtype):
    w = jax.nn.softmax(jnp.stack(lses, axis=0), axis=0)
    o = jnp.einsum('gnsh,gnshc->nshc', w, jnp.stack(outs, axis=0))
    n, s = o.shape[0], o.shape[1]
    return o.reshape(n, s, ATT_OUT).astype(dtype)

def short_conv(u_ext, conv_w):
    t = u_ext.shape[1] - (CONV_WIDTH - 1)
    z = u_ext[:, 0:t] * conv_w[0]
    for j in range(1, CONV_WIDTH):
        z = z + u_ext[:, j:j + t] * conv_w[j]
    return z

def peer_ffn(h, peer_w_q, peer_keys_1, peer_keys_2, peer_u, peer_v):
    n, s, d = h.shape
    tok = h.reshape(n * s, d)
    n_tok = n * s
    n_pad = -(-n_tok // PEER_CHUNK) * PEER_CHUNK
    tok = jnp.pad(tok, ((0, n_pad - n_tok), (0, 0)))
    half = PEER_D_KEY // 2
    k1 = peer_keys_1.astype(jnp.float32)
    k2 = peer_keys_2.astype(jnp.float32)

    def block(xc):
        qy = jnp.einsum('cd,de->ce', xc, peer_w_q).astype(jnp.float32)
        qy = qy.reshape(xc.shape[0], PEER_HEADS, PEER_D_KEY)
        s1 = jnp.einsum('chk,nk->chn', qy[..., :half], k1)
        s2 = jnp.einsum('chk,nk->chn', qy[..., half:], k2)
        v1, i1 = lax.top_k(s1, PEER_TOPK)
        v2, i2 = lax.top_k(s2, PEER_TOPK)
        cand = (v1[..., :, None] + v2[..., None, :]).reshape(xc.shape[0], PEER_HEADS, PEER_TOPK * PEER_TOPK)
        cid = (i1[..., :, None] * PEER_N_KEYS + i2[..., None, :]).reshape(xc.shape[0], PEER_HEADS, PEER_TOPK * PEER_TOPK)
        sc, pos = lax.top_k(cand, PEER_TOPK)
        eid = jnp.take_along_axis(cid, pos, axis=-1)
        g = jax.nn.softmax(sc, axis=-1)
        u = jnp.take(peer_u, eid, axis=0)
        act = jax.nn.gelu(jnp.einsum('cd,chkd->chk', xc, u).astype(jnp.float32), approximate=False)
        vv = jnp.take(peer_v, eid, axis=0)
        return jnp.einsum('chk,chkd->cd', (g * act).astype(xc.dtype), vv)

    out = lax.map(block, tok.reshape(n_pad // PEER_CHUNK, PEER_CHUNK, d))
    return out.reshape(n_pad, d)[:n_tok].reshape(n, s, d)

def finish_layer(x, y_att, z_conv, c_b, g_a, g_c, w_branch_attn, w_branch_conv, w_out,
                 ln1_g, ln1_b, peer_w_q, peer_keys_1, peer_keys_2, peer_u, peer_v, ln2_g, ln2_b):
    br_a = jnp.einsum('nse,ed->nsd', y_att, w_branch_attn)
    br_c = jnp.einsum('nse,ed->nsd', c_b * z_conv, w_branch_conv)
    merged = jax.nn.sigmoid(g_a) * br_a + jax.nn.sigmoid(g_c) * br_c
    mix = jnp.einsum('nsd,de->nse', merged, w_out)
    h = layer_norm(DEEPNORM_ALPHA * x + mix, ln1_g, ln1_b)
    f = peer_ffn(h, peer_w_q, peer_keys_1, peer_keys_2, peer_u, peer_v)
    return layer_norm(DEEPNORM_ALPHA * h + f, ln2_g, ln2_b)

def setup_inputs(seed: int = 0) -> dict:
    key = jax.random.key(seed)
    ks = jax.random.split(key, 24)

    def nrm(k, shape, scale):
        return jax.random.normal(k, shape, jnp.float32) * scale

    x_prompt = nrm(ks[0], (BATCH, SEQ, D_MODEL), 1.0)
    x_sample = nrm(ks[1], (DEC_BATCH, DEC_SEQ, D_MODEL), 1.0)
    cache_kv_w128 = nrm(ks[2], (DEPTH, DEC_BATCH, min(128, PAST_LEN), 2, N_SLOTS, HEAD_DIM), 1.0)
    cache_kv_w512 = nrm(ks[3], (DEPTH, DEC_BATCH, min(512, PAST_LEN), 2, N_SLOTS, HEAD_DIM), 1.0)
    cache_kv_w2048 = nrm(ks[4], (DEPTH, DEC_BATCH, min(2048, PAST_LEN), 2, N_SLOTS, HEAD_DIM), 1.0)
    state_conv = nrm(ks[5], (DEPTH, DEC_BATCH, CONV_WIDTH - 1, D_CONV), 1.0)
    w_qk = nrm(ks[6], (DEPTH, D_MODEL, 2 * ATT_W), D_MODEL ** -0.5)
    w_v = nrm(ks[7], (DEPTH, D_MODEL, ATT_W), D_MODEL ** -0.5 * DEEPNORM_BETA)
    w_rest = nrm(ks[8], (DEPTH, D_MODEL, 3 * D_CONV + 2 * D_MODEL), D_MODEL ** -0.5)
    w_in = jnp.concatenate([w_qk, w_v, w_rest], axis=-1)
    conv_w = nrm(ks[9], (DEPTH, CONV_WIDTH, D_CONV), CONV_WIDTH ** -0.5)
    w_branch_attn = nrm(ks[10], (DEPTH, ATT_OUT, D_MODEL), ATT_OUT ** -0.5)
    w_branch_conv = nrm(ks[11], (DEPTH, D_CONV, D_MODEL), D_CONV ** -0.5)
    w_out = nrm(ks[12], (DEPTH, D_MODEL, D_MODEL), D_MODEL ** -0.5 * DEEPNORM_BETA)
    ln1_g = 1.0 + nrm(ks[13], (DEPTH, D_MODEL), 0.05)
    ln1_b = nrm(ks[14], (DEPTH, D_MODEL), 0.02)
    peer_w_q = nrm(ks[15], (DEPTH, D_MODEL, PEER_HEADS * PEER_D_KEY), D_MODEL ** -0.5)
    peer_keys_1 = nrm(ks[16], (DEPTH, PEER_N_KEYS, PEER_D_KEY // 2), (PEER_D_KEY // 2) ** -0.5)
    peer_keys_2 = nrm(ks[17], (DEPTH, PEER_N_KEYS, PEER_D_KEY // 2), (PEER_D_KEY // 2) ** -0.5)
    peer_u = nrm(ks[18], (DEPTH, PEER_N_EXPERTS, D_MODEL), D_MODEL ** -0.5)
    peer_v = nrm(ks[19], (DEPTH, PEER_N_EXPERTS, D_MODEL), DEEPNORM_BETA)
    ln2_g = 1.0 + nrm(ks[20], (DEPTH, D_MODEL), 0.05)
    ln2_b = nrm(ks[21], (DEPTH, D_MODEL), 0.02)
    return {"x_prompt": x_prompt, "x_sample": x_sample,
            "cache_kv_w128": cache_kv_w128, "cache_kv_w512": cache_kv_w512,
            "cache_kv_w2048": cache_kv_w2048, "state_conv": state_conv,
            "w_in": w_in, "conv_w": conv_w, "w_branch_attn": w_branch_attn,
            "w_branch_conv": w_branch_conv, "w_out": w_out, "ln1_g": ln1_g, "ln1_b": ln1_b,
            "peer_w_q": peer_w_q, "peer_keys_1": peer_keys_1, "peer_keys_2": peer_keys_2,
            "peer_u": peer_u, "peer_v": peer_v, "ln2_g": ln2_g, "ln2_b": ln2_b}

def reference(x_prompt, x_sample, cache_kv_w128, cache_kv_w512, cache_kv_w2048, state_conv,
              w_in, conv_w, w_branch_attn, w_branch_conv, w_out, ln1_g, ln1_b,
              peer_w_q, peer_keys_1, peer_keys_2, peer_u, peer_v, ln2_g, ln2_b):
    caches = (cache_kv_w128, cache_kv_w512, cache_kv_w2048)
    seq = x_prompt.shape[1]
    dec_seq = x_sample.shape[1]
    pos_p = jnp.arange(seq)
    pos_s = PAST_LEN + jnp.arange(dec_seq)
    xp, xs = x_prompt, x_sample
    kv_p = [[], [], []]
    kv_s = [[], [], []]
    conv_p = []
    conv_s = []
    for layer in range(DEPTH):
        tail = (w_branch_attn[layer], w_branch_conv[layer], w_out[layer], ln1_g[layer], ln1_b[layer],
                peer_w_q[layer], peer_keys_1[layer], peer_keys_2[layer], peer_u[layer], peer_v[layer],
                ln2_g[layer], ln2_b[layer])

        q, k, v, u, c_b, g_a, g_c = mixer_projections(xp, pos_p, w_in[layer])
        outs, lses = [], []
        for gi, (win, dil) in enumerate(DIL_GROUPS):
            o, lse = dilated_band_attention(q[:, :, gi], k[:, :, gi], v[:, :, gi], dil, win // dil)
            outs.append(o)
            lses.append(lse)
            keep = min(win, seq)
            kv_p[gi].append(jnp.stack([k[:, seq - keep:, gi], v[:, seq - keep:, gi]], axis=2))
        y_att = combine_groups(outs, lses, xp.dtype)
        u_ext = jnp.pad(u, ((0, 0), (CONV_WIDTH - 1, 0), (0, 0)))
        z_conv = short_conv(u_ext, conv_w[layer])
        conv_p.append(u_ext[:, u_ext.shape[1] - (CONV_WIDTH - 1):])
        xp_next = finish_layer(xp, y_att, z_conv, c_b, g_a, g_c, *tail)

        q, k, v, u, c_b, g_a, g_c = mixer_projections(xs, pos_s, w_in[layer])
        outs, lses = [], []
        for gi, (win, dil) in enumerate(DIL_GROUPS):
            buf = caches[gi][layer]
            n_prev = buf.shape[1]
            k_all = jnp.concatenate([buf[:, :, 0], k[:, :, gi]], axis=1)
            v_all = jnp.concatenate([buf[:, :, 1], v[:, :, gi]], axis=1)
            o, lse = dilated_cached_attention(q[:, :, gi], k_all, v_all, n_prev, dil, win // dil)
            outs.append(o)
            lses.append(lse)
            n_all = k_all.shape[1]
            kv_s[gi].append(jnp.stack([k_all[:, n_all - n_prev:], v_all[:, n_all - n_prev:]], axis=2))
        y_att = combine_groups(outs, lses, xs.dtype)
        u_ext = jnp.concatenate([state_conv[layer].astype(u.dtype), u], axis=1)
        z_conv = short_conv(u_ext, conv_w[layer])
        conv_s.append(u_ext[:, u_ext.shape[1] - (CONV_WIDTH - 1):])
        xs_next = finish_layer(xs, y_att, z_conv, c_b, g_a, g_c, *tail)

        xp, xs = xp_next, xs_next

    return (xp, xs,
            jnp.stack(kv_p[0]), jnp.stack(kv_p[1]), jnp.stack(kv_p[2]), jnp.stack(conv_p),
            jnp.stack(kv_s[0]), jnp.stack(kv_s[1]), jnp.stack(kv_s[2]), jnp.stack(conv_s))


_drawn_inputs = setup_inputs


def setup_inputs(seed=0):
    import zlib

    import numpy as np

    out = dict(_drawn_inputs(seed))
    spreads = {}
    factors = {'ln2_b': 2.755}
    for name, (base, spread) in spreads.items():
        noise = np.random.default_rng([zlib.crc32(name.encode()), seed]).standard_normal(out[name].shape)
        drawn = base * np.exp(spread * noise) if base else spread * noise
        out[name] = __import__('jax').numpy.asarray(drawn.astype(out[name].dtype))
    for name, factor in factors.items():
        out[name] = (out[name] * factor).astype(out[name].dtype)
    return out
```

```python
import math
from contextlib import ExitStack

import numpy as np

import concourse.bass as bass
from concourse import mybir
from concourse.alu_op_type import AluOpType as ALU

ACT = mybir.ActivationFunctionType
F32 = mybir.dt.float32
F32R = mybir.dt.float32r
BF16 = mybir.dt.bfloat16
U32 = mybir.dt.uint32
AX = mybir.AxisListType

P = 128
D = 1024
KD = D // P
SEQ = 1024
DB, DS = 8, 8
NS = DB * DS
T = SEQ + NS
NT = (T + P - 1) // P
PT = SEQ // P
SLOTS, HD, NG = 8, 64, 3
AW = SLOTS * HD
ATT_W = NG * AW
SP = SLOTS // 2
GROUPS = ((128, 1), (512, 4), (2048, 16))
PREV = (128, 512, 1024)
CHUNKS = ((0, 384), (384, 384), (768, 320))
ALPHA = 2.0 ** 0.25
EPS = 1e-5
SCALE = HD ** -0.5
HEADS, KEYS, TOPK = 8, 128, 16
NEG = -1e30
LOW = -3.0e38
C_CONV = 3 * ATT_W


def rows_of(t):
    return min(P, T - P * t)


def split3(pe, out, lh, ll, rh, rl, first, last):
    pe.matmul(out, lh, rh, start=first, stop=False)
    pe.matmul(out, lh, rl, start=False, stop=False)
    return pe.matmul(out, ll, rh, start=False, stop=last)


def load_x(nc, io, k):
    with ExitStack() as c:
        xin = c.enter_context(nc.sbuf_tensor("xin", [P, 2, D], F32))
        ps = c.enter_context(nc.psum_tensor("x_ps", [P, 2, D], F32))
        x_in = [nc.alloc_semaphore(f"x_in{b}") for b in range(2)]
        x_turned, x_hi, x_lo = (nc.alloc_semaphore(n) for n in ("x_turned", "x_hi", "x_lo"))
        consts = nc.alloc_semaphore("consts_in")
        block = c.enter_context(nc.Block())

        def tile(t):
            src = io["x_prompt"][0, t * P:(t + 1) * P] if t < PT else io["x_sample"].rearrange("b s d -> (b s) d")
            return src

        @block.sync
        def _(sp):
            sp.dma_start(k["ident"][:], io["c_ident"]).then_inc(consts, 16)
            for t in range(NT):
                if t >= 2:
                    sp.wait_ge(x_turned, t - 1)
                sp.dma_start(xin[:rows_of(t), t % 2], tile(t)).then_inc(x_in[t % 2], 16)

        @block.tensor
        def _(pe):
            pe.wait_ge(consts, 16)
            for t in range(NT):
                n = rows_of(t)
                pe.wait_ge(x_in[t % 2], 16 * (t // 2 + 1))
                if t >= 2:
                    pe.wait_ge(x_lo, t - 1)
                for j in range(KD):
                    m = pe.transpose(ps[:, t % 2, j * P:j * P + n], xin[:n, t % 2, j * P:(j + 1) * P], k["ident"][:n, :n])
                m.then_inc(x_turned, 1)

        @block.scalar
        def _(act):
            for t in range(NT):
                n = rows_of(t)
                act.wait_ge(x_turned, t + 1)
                act.activation(k["xTh"][:, :, t * P:t * P + n],
                               ps[:, t % 2].rearrange("p (j n) -> p j n", j=KD)[:, :, :n], ACT.Copy).then_inc(x_hi, 1)

        @block.vector
        def _(dve):
            for t in range(NT):
                n = rows_of(t)
                dve.wait_ge(x_hi, t + 1)
                dve.tensor_tensor(k["xTl"][:, :, t * P:t * P + n],
                                  ps[:, t % 2].rearrange("p (j n) -> p j n", j=KD)[:, :, :n],
                                  k["xTh"][:, :, t * P:t * P + n].bitcast(F32), ALU.subtract).then_inc(x_lo, 1)


def key_tiles(i):
    return [(0, max(0, i - 1)), (1, max(0, i - 4)), (2, 0)]


def prompt_attn(nc, io, k):
    W3 = NG * P
    MW = (2 + 5 + PT) * P
    MOFF = (0, 2 * P, 7 * P, MW)
    units = [(i, h) for i in range(PT) for h in range(2)]
    NU = len(units)

    def width(i):
        return sum(i + 1 - f for _, f in key_tiles(i)) * P

    chunks = []
    for u, (i, h) in enumerate(units):
        nb = width(i) // P
        chunks += [(u, b, min(4, nb - b)) for b in range(0, nb, 4)]
    NCA, NCD = (len(chunks) + 1) // 2, len(chunks) // 2

    with ExitStack() as c:
        def sb(n, s, d=F32):
            return c.enter_context(nc.sbuf_tensor(n, s, d))

        def sem(n):
            return nc.alloc_semaphore(n)

        raw = sb("w_raw", [P, 2, 4, W3])
        wh, wl = sb("w_hi", [P, KD, W3], F32R), sb("w_lo", [P, KD, W3], F32R)
        cos, sin = sb("cos", [P, NT, 32]), sb("sin", [P, NT, 2, 32])
        mask = sb("mask", [P, MW])
        qR, kR, vR = sb("qR", [P, 2, W3]), sb("kR", [P, NT, W3]), sb("vR", [P, NT, W3])
        tmp = sb("rope_tmp", [P, 2, W3])
        tick = sb("tick", [P, 1])
        qT, kT = sb("qT", [P, NG, SEQ]), sb("kT", [P, NG, SEQ])
        S = sb("S", [P, 2, MW])
        PTs = sb("PTs", [P, MW])
        m3, nm, den, rden = sb("m3", [P, 2, NG]), sb("nm", [P, 2]), sb("den", [P, 2]), sb("rden", [P, 2])
        Os = sb("Os", [P, 2, P])
        attS = sb("attS", [P, SEQ])
        ps = c.enter_context(nc.psum_tensor("a_ps", [P, 8, 512], F32))
        psS = ps[:, 0:4].rearrange("p b n -> p (b n)")

        raw_in = [sem(f"raw_in{b}") for b in range(2)]
        w_hi_done = sem("w_hi_done")
        w_lo_done = sem("w_lo_done")
        z_ready = sem("z_ready")
        z_free = sem("z_free")
        rot_done = sem("rot_done")
        turned = sem("turned")
        turn_free = sem("turn_free")
        kv_out, kv_flushed = sem("kv_out"), sem("kv_flushed")
        s_ready = sem("s_ready")
        s_free = sem("s_free")
        sm_ready, p_ready = sem("sm_ready"), sem("p_ready")
        pt_ready = [sem("ptA_ready"), sem("ptD_ready")]
        pt_done = [sem("ptA_done"), sem("ptD_done")]
        o_ready = sem("o_ready")
        o_normed = sem("o_normed")
        ot_ready = sem("ot_ready")
        ot_done = sem("ot_done")
        att_out, att_stored = sem("att_out"), sem("att_stored")
        consts = sem("a_consts")
        block = c.enter_context(nc.Block())

        w_view = io["w_in"][0][:, :3 * ATT_W].rearrange("(f k p) (r g s c) -> r s f k p g c", f=2, k=4, r=3, g=NG, s=SP)
        kv_prompt = [io[f"o_kv{g}_prompt"] for g in range(NG)]
        kv_sample = [io[f"o_kv{g}_sample"] for g in range(NG)]
        ZT = 3 * NT

        @block.sync
        def _(sp):
            sp.dma_start(cos[:], io["c_cos"].rearrange("p (t c) -> p t c", t=NT)).then_inc(consts, 16)
            sp.dma_start(sin[:], io["c_sin"].rearrange("p (t a c) -> p t a c", t=NT, a=2)).then_inc(consts, 16)
            sp.dma_start(mask[:], io["c_mask_prompt"]).then_inc(consts, 16)
            sp.sem_inc(kv_flushed, 1)
            with sp.Fori(0, SP) as s:
                for r in range(3):
                    for f in range(2):
                        sp.wait_ge(w_lo_done, s * 6 + (2 * r + f + 1))
                        for kk in range(4):
                            sp.dma_start(raw[:, f, kk].rearrange("p (g c) -> p g c", g=NG),
                                         w_view[r, s, f, kk]).then_inc(raw_in[f], 16)
                sp.wait_ge(z_free, s * ZT + (ZT + 3))
                for which, buf in ((0, kR), (1, vR)):
                    for g in range(NG):
                        first = (SEQ - min(GROUPS[g][0], SEQ)) // P
                        cols = slice(g * P, (g + 1) * P)
                        dst = kv_prompt[g][0, 0, :, which].rearrange("(t p) (s j) e -> s p t (j e)", p=P, j=2)[s]
                        sp.dma_start(dst, buf[:, first:PT, cols]).then_inc(kv_out, 16)
                        dst = kv_sample[g][0, :, PREV[g] - DS:, which].rearrange("b r (s j) e -> s b r (j e)", j=2)[s]
                        sp.dma_start(dst, buf[:NS, PT, cols]).then_inc(kv_out, 16)
                for which, buf in ((0, qR[:NS, PT % 2]), (1, kR[:NS, PT]), (2, vR[:NS, PT])):
                    dst = io["s_qkv"][which].rearrange("g b r (s c) -> s (b r) g c", s=SP)[s]
                    sp.dma_start(dst, buf.rearrange("p (g c) -> p g c", g=NG)).then_inc(kv_out, 16)
                sp.wait_ge(kv_out, (s + 1) * (16 * (4 * NG + 3)))
                sp.sem_inc(kv_flushed, 1)

        @block.gpsimd
        def _(pool):
            pool.sem_inc(att_stored, 1)
            with pool.Fori(0, SP) as s:
                pool.wait_ge(w_lo_done, s * 6 + 6)
                for g, name in enumerate(("cache_kv_w128", "cache_kv_w512", "cache_kv_w2048")):
                    pool.dma_start(
                        io[f"o_kv{g}_sample"][0, :, :PREV[g] - DS].rearrange("(s b) r w s2 e -> s b (r w s2 e)", b=DB // SP)[s],
                        io[name][0, :, DS:].rearrange("(s b) r w s2 e -> s b (r w s2 e)", b=DB // SP)[s]
                    ).then_inc(k["cache_moved"], 16)
                pool.wait_ge(ot_done, s * PT + (PT + 1))
                pool.dma_start(io["s_att"][s][:, :SEQ], attS[:]).then_inc(att_out, 16)
                pool.wait_ge(att_out, (s + 1) * 16)
                pool.sem_inc(att_stored, 1)

        @block.scalar
        def _(act):
            act.sem_inc(turn_free, 2)
            act.sem_inc(pt_done[0], 1)
            act.sem_inc(ot_done, 1)
            with act.Fori(0, SP) as s:
                for r in range(3):
                    act.wait_ge(z_ready, s * ZT + (r * NT + 1))
                    for f in range(2):
                        act.wait_ge(raw_in[f], (s * 3 + (r + 1)) * 64)
                        act.activation(wh[:, 4 * f:4 * f + 4], raw[:, f], ACT.Copy).then_inc(w_hi_done, 1)
                    if r < 2:
                        for t in range(PT):
                            act.wait_ge(turned, s * (2 * PT) + (r * PT + t + 1))
                            act.activation((qT, kT)[r][:, :, t * P:(t + 1) * P],
                                           ps[:, 4 + t % 2, :W3].rearrange("p (g n) -> p g n", g=NG),
                                           ACT.Copy).then_inc(turn_free, 1)

                def exp(u):
                    b, w = u % 2, width(units[u][0])
                    act.wait_ge(sm_ready, s * NU + (u + 1))
                    act.activation(S[:, b, :w], S[:, b, :w], ACT.Exp, bias=nm[:, b:b + 1],
                                   accum_out=den[:, b:b + 1]).then_inc(p_ready, 1)

                def copy_turned(u):
                    for q, (uu, b0, nb) in enumerate(chunks):
                        if uu == u and q % 2 == 0:
                            act.wait_ge(pt_ready[0], s * NCA + (q // 2 + 1))
                            act.activation(PTs[:, b0 * P:(b0 + nb) * P], ps[:, 4, :nb * P],
                                           ACT.Copy).then_inc(pt_done[0], 1)

                def turned_out(i):
                    act.wait_ge(ot_ready, s * PT + (i + 1))
                    if i == 0:
                        act.wait_ge(att_stored, s + 1)
                    act.activation(attS[:, i * P:(i + 1) * P], ps[:, 7, P:2 * P], ACT.Copy).then_inc(ot_done, 1)

                exp(0)
                for u in range(NU):
                    if u + 1 < NU:
                        exp(u + 1)
                    copy_turned(u)
                    if u >= 2 and u % 2 == 0:
                        turned_out(u // 2 - 1)
                turned_out(PT - 1)

        @block.vector
        def _(dve):
            dve.wait_ge(consts, 48)
            dve.sem_inc(w_lo_done, 2)
            dve.sem_inc(z_free, 3)
            dve.sem_inc(s_free, 1)
            dve.sem_inc(pt_done[1], 1)
            dve.sem_inc(o_normed, 2)
            with dve.Fori(0, SP) as s:
                dve.wait_ge(kv_flushed, s + 1)
                for r in range(3):
                    for f in range(2):
                        dve.wait_ge(w_hi_done, s * 6 + (2 * r + f + 1))
                        dve.tensor_tensor(wl[:, 4 * f:4 * f + 4], raw[:, f], wh[:, 4 * f:4 * f + 4].bitcast(F32),
                                          ALU.subtract).then_inc(w_lo_done, 1)
                    for t in range(NT):
                        n = rows_of(t)
                        z = ps[:n, t % 3, :W3]
                        dve.wait_ge(z_ready, s * ZT + (r * NT + t + 2))
                        if r == 2:
                            dve.tensor_copy(vR[:n, t], z).then_inc(z_free, 1)
                            continue
                        if r == 0 and t >= 2:
                            dve.wait_ge(turned, s * (2 * PT) + (t - 1))
                        out = (qR[:n, t % 2] if r == 0 else kR[:n, t]).rearrange("p (h a c) -> p h a c", a=2, c=32)
                        z4 = z.rearrange("p (h a c) -> p h a c", a=2, c=32)
                        t4 = tmp[:n, t % 2].rearrange("p (h a c) -> p h a c", a=2, c=32)
                        dve.tensor_tensor(t4, z4, cos[:n, t].unsqueeze(1).unsqueeze(1).to_broadcast([n, 2 * NG, 2, 32]), ALU.mult)
                        for a in range(2):
                            m = dve.tensor_tensor(out[:, :, a], z4[:, :, 1 - a],
                                                  sin[:n, t, a].unsqueeze(1).to_broadcast([n, 2 * NG, 32]), ALU.mult)
                        m.then_inc(z_free, 1)
                        dve.drain()
                        dve.tensor_tensor(out, out, t4, ALU.add).then_inc(rot_done, 1)

                def mask_scores(u):
                    i, h = units[u]
                    b, off = u % 2, 0
                    dve.wait_ge(s_ready, s * NU + (u + 1))
                    dve.memset(tick[:], 0.0)
                    for g, first in key_tiles(i):
                        w = (i + 1 - first) * P
                        m = dve.tensor_tensor_reduce(S[:, b, off:off + w], psS[:, off:off + w],
                                                     mask[:, MOFF[g + 1] - w:MOFF[g + 1]], SCALE, LOW,
                                                     ALU.add, ALU.max, m3[:, b, g:g + 1])
                        off += w
                    m.then_inc(s_free, 1)
                    dve.drain()
                    dve.tensor_reduce(nm[:, b:b + 1], m3[:, b], AX.X, ALU.max, negate=True).then_inc(sm_ready, 1)

                def copy_turned(u):
                    for q, (uu, b0, nb) in enumerate(chunks):
                        if uu == u and q % 2 == 1:
                            dve.wait_ge(pt_ready[1], s * NCD + (q // 2 + 1))
                            dve.tensor_copy(PTs[:, b0 * P:(b0 + nb) * P], ps[:, 5, :nb * P]).then_inc(pt_done[1], 1)

                def normalise(u):
                    i, h = units[u]
                    b = u % 2
                    dve.reciprocal(rden[:, b:b + 1], den[:, b:b + 1])
                    dve.drain()
                    dve.wait_ge(o_ready, s * NU + (u + 1))
                    dve.tensor_scalar(Os[:, i % 2, h * HD:(h + 1) * HD],
                                      ps[:, 6 + b, :HD],
                                      rden[:, b:b + 1], None, ALU.mult).then_inc(o_normed, 1)

                mask_scores(0)
                for u in range(NU):
                    if u + 1 < NU:
                        mask_scores(u + 1)
                    copy_turned(u)
                    dve.wait_ge(p_ready, s * NU + (u + 1))
                    normalise(u)

        @block.tensor
        def _(pe):
            pe.sem_inc(z_ready, 1)
            with pe.Fori(0, SP) as s:
                pe.wait_ge(s_free, s * NU + 1)
                for b in range(2):
                    pe.wait_ge(pt_done[b], s * (NCA, NCD)[b] + 1)

                def turn(r, t):
                    src = qR[:, t % 2] if r == 0 else kR[:, t]
                    pe.wait_ge(rot_done, s * (2 * NT) + (r * NT + t + 1))
                    pe.wait_ge(turn_free, s * (2 * PT) + (r * PT + t + 1))
                    for g in range(NG):
                        m = pe.transpose(ps[:, 4 + t % 2, g * P:(g + 1) * P], src[:, g * P:(g + 1) * P], k["ident"][:])
                    m.then_inc(turned, 1)

                for r in range(3):
                    pe.wait_ge(w_lo_done, s * 6 + (2 * r + 4))
                    for t in range(NT):
                        n = rows_of(t)
                        pe.wait_ge(z_free, s * ZT + (r * NT + t + 1))
                        for kk in range(KD):
                            m = split3(pe, ps[:n, t % 3, :W3], k["xTh"][:, kk, t * P:t * P + n],
                                       k["xTl"][:, kk, t * P:t * P + n], wh[:, kk], wl[:, kk], kk == 0, kk == KD - 1)
                        m.then_inc(z_ready, 1)
                        if r < 2 and t >= 1:
                            turn(r, t - 1)

                def scores(u):
                    i, h = units[u]
                    pe.wait_ge(s_free, s * NU + (u + 1))
                    off = 0
                    for g, first in key_tiles(i):
                        key, end = first * P, (i + 1) * P
                        while key < end:
                            w = min(end - key, 512 - off % 512)
                            m = pe.matmul(psS[:, off:off + w], qT[h * HD:(h + 1) * HD, g, i * P:(i + 1) * P],
                                          kT[h * HD:(h + 1) * HD, g, key:key + w], start=True, stop=True)
                            key, off = key + w, off + w
                    m.then_inc(s_ready, 1)

                def weigh_values(u):
                    i, h = units[u]
                    blocks = [(g, j) for g, first in key_tiles(i) for j in range(first, i + 1)]
                    pe.wait_ge(p_ready, s * NU + (u + 1))
                    mine = [(q, b0, nb) for q, (uu, b0, nb) in enumerate(chunks) if uu == u]

                    def turn_chunk(q, b0, nb):
                        pe.wait_ge(pt_done[q % 2], s * (NCA, NCD)[q % 2] + (q // 2 + 1))
                        for x in range(nb):
                            m = pe.transpose(ps[:, 4 + q % 2, x * P:(x + 1) * P],
                                             S[:, u % 2, (b0 + x) * P:(b0 + x + 1) * P], k["ident"][:])
                        m.then_inc(pt_ready[q % 2], 1)

                    def use_chunk(q, b0, nb):
                        pe.wait_ge(pt_done[q % 2], s * (NCA, NCD)[q % 2] + (q // 2 + 2))
                        for x in range(b0, b0 + nb):
                            g, j = blocks[x]
                            m = pe.matmul(ps[:, 6 + u % 2, :HD],
                                          PTs[:, x * P:(x + 1) * P], vR[:, j, g * P + h * HD:g * P + (h + 1) * HD],
                                          start=(x == 0), stop=(x == len(blocks) - 1))
                        return m

                    pe.wait_ge(o_normed, s * NU + (u + 1))
                    if h == 1:
                        pe.wait_ge(ot_done, s * PT + (i + 1))
                    turn_chunk(*mine[0])
                    for x in range(len(mine)):
                        if x + 1 < len(mine):
                            turn_chunk(*mine[x + 1])
                        m = use_chunk(*mine[x])
                    m.then_inc(o_ready, 1)

                def turn_out(i):
                    pe.wait_ge(o_normed, s * NU + (2 * i + 4))
                    pe.transpose(ps[:, 7, P:2 * P], Os[:, i % 2], k["ident"][:]).then_inc(ot_ready, 1)

                pe.wait_ge(z_free, s * ZT + (ZT + 3))
                pe.wait_ge(turn_free, s * (2 * PT) + (2 * PT + 2))
                scores(0)
                for u in range(NU):
                    if u + 1 < NU:
                        scores(u + 1)
                    weigh_values(u)
                    if u >= 2 and u % 2 == 0:
                        turn_out(u // 2 - 1)
                turn_out(PT - 1)


def sample_attn(nc, io, k):
    CT = 9
    NEW = NG * DS
    W = CT * P + NEW
    COL = [0] + [P + NEW + P * j for j in range(CT - 1)]
    R = SLOTS * DS
    with ExitStack() as c:
        def sb(n, s, d=F32):
            return c.enter_context(nc.sbuf_tensor(n, s, d))

        def sem(n):
            return nc.alloc_semaphore(n)

        C = sb("cache", [P, 2, CT, 2 * AW])
        new = sb("new", [NEW, 2, 3, AW])
        KT = sb("KT", [P, SP, W])
        QB = sb("QB", [P, NG, SP * 80])
        S = sb("Ss", [R, W])
        mask = sb("smask", [R, W])
        PTs = sb("PTss", [P, CT + 1, R])
        mx, nm, den, rden = sb("mx", [R, 1]), sb("snm", [R, 1]), sb("sden", [R, 1]), sb("srden", [R, 1])
        tick = sb("stick", [P, 1])
        att = sb("att_new", [P, SP, NS])
        ps = c.enter_context(nc.psum_tensor("b_ps", [P, 8, 512], F32))
        S0 = 3 * 512 + 512 - P - NEW
        flat = ps.rearrange("p b n -> p (b n)")

        cache_in = [sem(f"cache_in{b}") for b in range(2)]
        pv_done = sem("pv_done")
        st_ready, st_done = sem("st_ready"), sem("st_done")
        kt_ready = [sem("ktA_ready"), sem("ktD_ready")]
        kt_done = [sem("ktA_done"), sem("ktD_done")]
        s_ready, sm_ready, p_exp, p_ready = sem("ss_ready"), sem("ssm_ready"), sem("sp_exp"), sem("sp_ready")
        pt_ready, pt_act, pt_dve = sem("spt_ready"), sem("spt_act"), sem("spt_dve")
        o_done = sem("so_done")
        out_sem, consts = sem("b_out"), sem("b_consts")
        block = c.enter_context(nc.Block())
        NA, ND = (CT + 1) // 2, CT // 2

        caches = [io["cache_kv_w128"], io["cache_kv_w512"], io["cache_kv_w2048"]]
        rows = [x[0].rearrange("b r w s e -> b r (w s e)") for x in caches]

        @block.sync
        def _(sp):
            sp.dma_start(mask[:], io["c_mask_sample"]).then_inc(consts, 16)
            with sp.Fori(0, DB // 2) as q:
                for x in range(2):
                    b = q * 2 + x
                    sp.wait_ge(pv_done, b + 1)
                    sp.dma_start(C[:, x, 0], rows[0][b]).then_inc(cache_in[x], 16)
                    sp.dma_start(C[:, x, 1:5], rows[1][b].rearrange("(t p) e -> p t e", p=P)).then_inc(cache_in[x], 16)
                    far = rows[2][b].rearrange("(m a r) e -> m a r e", m=4, r=16)[:, :, :DS]
                    for m in range(4):
                        sp.dma_start(C[:, x, 5 + m], far[m]).then_inc(cache_in[x], 16)
                    for w in range(3):
                        sp.dma_start(new[:, x, w], io["s_qkv"][w, :, b]).then_inc(cache_in[x], 16)
            sp.wait_ge(o_done, DB + 1)
            sp.dma_start(io["s_att"].rearrange("s p n -> p s n")[:, :, SEQ:], att[:]).then_inc(out_sem, 16)
            sp.wait_ge(out_sem, 16)

        @block.gpsimd
        def _(pool):
            pool.memset(QB[:], 0.0).then_inc(consts, 1)

        @block.scalar
        def _(act):
            act.sem_inc(kt_done[0], 1)
            with act.Fori(0, DB) as b:
                act.wait_ge(st_ready, b + 1)
                st = ps[:, 2, :2 * SP * NEW].rearrange("p (w s n) -> p w s n", w=2, s=SP)
                act.activation(KT[:, :, P:P + NEW], st[:, 1], ACT.Copy)
                for h in range(2):
                    rng = slice(h * HD, (h + 1) * HD)
                    m = act.activation(
                        QB[rng].rearrange("p g (s w) -> p s g w", w=80)[:, :, :, h * DS:(h + 1) * DS],
                        st[rng, 0].rearrange("p s (g t) -> p s g t", g=NG), ACT.Copy)
                m.then_inc(st_done, 1)
                for j in range(0, CT, 2):
                    act.wait_ge(kt_ready[0], b * NA + (j // 2 + 1))
                    act.activation(KT[:, :, COL[j]:COL[j] + P], ps[:, 0].rearrange("p (s n) -> p s n", s=SP),
                                   ACT.Copy).then_inc(kt_done[0], 1)
                act.wait_ge(sm_ready, b + 1)
                act.activation(S[:], S[:], ACT.Exp, bias=nm[:], accum_out=den[:]).then_inc(p_exp, 1)
                act.wait_ge(pt_ready, b + 1)
                act.activation(PTs[:, 0:5], ps[:, 6, :5 * R].rearrange("p (j r) -> p j r", j=5),
                               ACT.Copy).then_inc(pt_act, 1)

        @block.vector
        def _(dve):
            dve.sem_inc(kt_done[1], 1)
            dve.sem_inc(o_done, 1)
            dve.wait_ge(consts, 17)
            with dve.Fori(0, DB) as b:
                for j in range(1, CT, 2):
                    dve.wait_ge(kt_ready[1], b * ND + (j // 2 + 1))
                    dve.tensor_copy(KT[:, :, COL[j]:COL[j] + P],
                                    ps[:, 1].rearrange("p (s n) -> p s n", s=SP)).then_inc(kt_done[1], 1)
                dve.wait_ge(s_ready, b + 1)
                dve.memset(tick[:], 0.0)
                dve.tensor_tensor_reduce(S[:], flat[:R, S0:S0 + W], mask[:], SCALE, LOW, ALU.add, ALU.max, mx[:])
                dve.drain()
                dve.tensor_scalar(nm[:], mx[:], -1.0, None, ALU.mult).then_inc(sm_ready, 1)
                dve.wait_ge(p_exp, b + 1)
                dve.reciprocal(rden[:], den[:])
                dve.drain()
                dve.tensor_scalar(S[:], S[:], rden[:], None, ALU.mult).then_inc(p_ready, 1)
                dve.wait_ge(pt_ready, b + 1)
                dve.tensor_copy(PTs[:, 5:CT], ps[:, 7, :4 * R].rearrange("p (j r) -> p j r", j=4))
                dve.tensor_copy(PTs[:NEW, CT], ps[:NEW, 7, 4 * R:5 * R]).then_inc(pt_dve, 1)
                dve.wait_ge(pv_done, b + 3)
                for h in range(2):
                    rng = slice(h * HD, (h + 1) * HD)
                    o = ps[rng, 2, 256:256 + 16 * SP].rearrange("p (s n) -> p s n", s=SP)[:, :, h * DS:(h + 1) * DS]
                    m = dve.tensor_copy(att[rng, :, bass.ds(b * DS, DS)], o)
                m.then_inc(o_done, 1)

        @block.tensor
        def _(pe):
            pe.sem_inc(pv_done, 2)
            ident = k["ident"]
            pe.wait_ge(consts, 17)
            with pe.Fori(0, DB // 2) as q:
                for x in range(2):
                    b = q * 2 + x
                    pe.wait_ge(cache_in[x], (q + 1) * 144)
                    pe.wait_ge(o_done, b + 1)

                    def turn_keys(j):
                        pe.wait_ge(kt_done[j % 2], b * (NA, ND)[j % 2] + (j // 2 + 1))
                        for s in range(SP):
                            m = pe.transpose(ps[:, j % 2, s * P:(s + 1) * P], C[:, x, j, s * P:(s + 1) * P], ident[:])
                        m.then_inc(kt_ready[j % 2], 1)

                    turn_keys(0)
                    for w in range(2):
                        for s in range(SP):
                            at = (w * SP + s) * NEW
                            m = pe.transpose(ps[:, 2, at:at + NEW], new[:, x, w, s * P:(s + 1) * P], ident[:NEW, :NEW])
                    m.then_inc(st_ready, 1)
                    for j in range(1, CT):
                        turn_keys(j)
                    pe.wait_ge(st_done, b + 1)
                    pe.wait_ge(kt_done[0], (b + 1) * NA + 1)
                    pe.wait_ge(kt_done[1], (b + 1) * ND + 1)
                    pieces = [(0, 0, P)] + [(g, P + g * DS, DS) for g in range(NG)] + [(1, COL[1], 512), (2, COL[5], 512)]
                    for g, at, w in pieces:
                        for s in range(SP):
                            m = pe.matmul(flat[:R, S0 + at:S0 + at + w], QB[:, g, s * 64:(s + 1) * 64],
                                          KT[:, s, at:at + w], start=(s == 0), stop=(s == SP - 1))
                    m.then_inc(s_ready, 1)
                    pe.wait_ge(p_ready, b + 1)
                    pe.matmul(ps[:, 6, :R], S[:, :P], ident[:R, :R], start=True, stop=True)
                    for j in range(1, CT):
                        pe.transpose(ps[:, 6 + j // 5, (j % 5) * R:(j % 5 + 1) * R], S[:, COL[j]:COL[j] + P], ident[:R, :R])
                    pe.transpose(ps[:NEW, 7, 4 * R:5 * R], S[:, P:P + NEW], ident[:R, :R]).then_inc(pt_ready, 1)
                    pe.wait_ge(pt_act, b + 1)
                    pe.wait_ge(pt_dve, b + 1)
                    for s in range(SP):
                        out = ps[:, 2, 256 + s * 16:256 + (s + 1) * 16]
                        cols = slice(AW + s * P, AW + (s + 1) * P)
                        for j in range(CT):
                            pe.matmul(out, C[:, x, j, cols], PTs[:, j, s * 16:(s + 1) * 16], start=(j == 0), stop=False)
                        m = pe.matmul(out, new[:, x, 2, s * P:(s + 1) * P], PTs[:NEW, CT, s * 16:(s + 1) * 16],
                                      start=False, stop=True)
                    m.then_inc(pv_done, 1)


def conv_gates(nc, io, k):
    UNITS = (0, 2, 1, 3, 4)
    NU, NC = len(UNITS), len(CHUNKS)
    NST = 2 * DB
    CS = NST + 3
    AJ, DJ = 3 * NC, 2 * NC
    with ExitStack() as c:
        def sb(n, s, d=F32):
            return c.enter_context(nc.sbuf_tensor(n, s, d))

        def sem(n):
            return nc.alloc_semaphore(n)

        raw = sb("c_raw", [P, 2, KD, P])
        wh, wl = sb("c_wh", [P, 2, KD, P], F32R), sb("c_wl", [P, 2, KD, P], F32R)
        rows, cs, csj = sb("cs_rows", [CS, D]), sb("cs", [P, KD, CS]), sb("csj", [P, CS])
        ci, z = sb("ci", [P, T]), sb("z", [P, T])
        up, us = sb("u_prompt", [P, 2 + SEQ]), sb("u_sample", [P, DB, 2 + DS])
        gate = sb("gate", [P, 2, T])
        ulast, urows = sb("ulast", [P, KD, 2 + NST]), sb("urows", [2 + NST, D])
        ps = c.enter_context(nc.psum_tensor("c_ps", [P, 8, 512], F32))

        raw_in = [sem(f"c_raw_in{b}") for b in range(2)]
        w_hi, w_lo = sem("c_w_hi"), sem("c_w_lo")
        z_ready = sem("c_z_ready")
        z_act, z_dve = sem("z_act"), sem("z_dve")
        gate_out = [sem(f"gate_out{x}") for x in range(2)]
        gate_free = sem("gate_free")
        rows_in, cs_ready, cs_done = sem("rows_in"), sem("cs_ready"), sem("cs_done")
        last_ready, last_done, last_out = sem("last_ready"), sem("last_done"), sem("last_out")
        j_done = sem("j_done")
        block = c.enter_context(nc.Block())
        w_view = io["w_in"][0][:, C_CONV:].rearrange("(k p) (m j c) -> m j p k c", k=KD, m=5, j=KD)

        @block.sync
        def _(sp):
            sp.dma_start(rows[:NST], io["state_conv"][0].rearrange("b t d -> (b t) d")).then_inc(rows_in, 16)
            sp.dma_start(rows[NST:], io["conv_w"][0]).then_inc(rows_in, 16)
            with sp.Fori(0, KD // 2) as q:
                for i in range(2 * NU):
                    sp.wait_ge(w_lo, q * (2 * NU) + (i + 1))
                    sp.dma_start(raw[:, i % 2], w_view[UNITS[i % NU], q * 2 + i // NU]).then_inc(raw_in[i % 2], 16)
            sp.wait_ge(last_done, 2)
            sp.dma_start(io["o_conv_prompt"][0, 0], urows[:2]).then_inc(last_out, 16)
            sp.dma_start(io["o_conv_sample"][0].rearrange("b t d -> (b t) d"), urows[2:]).then_inc(last_out, 16)
            sp.wait_ge(last_out, 32)

        @block.gpsimd
        def _(pool):
            pool.sem_inc(gate_free, 2)
            with pool.Fori(0, KD) as j:
                for x in range(2):
                    pool.wait_ge(z_act, j * AJ + ((2 + x) * NC + AJ))
                    pool.dma_start(io["s_gate"][x][j], gate[:, x]).then_inc(gate_out[x], 16)
                for x in range(2):
                    pool.wait_ge(gate_out[x], (j + 1) * 16)
                    pool.sem_inc(gate_free, 1)

        @block.scalar
        def _(act):
            act.sem_inc(z_act, AJ)
            act.wait_ge(cs_ready, 1)
            act.activation(cs[:], ps[:, 7, :KD * CS].rearrange("p (j s) -> p j s", j=KD), ACT.Copy).then_inc(cs_done, 1)
            with act.Fori(0, KD // 2) as q:
                def split(i):
                    act.wait_ge(raw_in[i % 2], (q * NU + (i // 2 + 1)) * 16)
                    act.wait_ge(z_ready, q * (2 * NU * NC) + (NC * i + NC))
                    act.activation(wh[:, i % 2], raw[:, i % 2], ACT.Copy).then_inc(w_hi, 1)

                split(0)
                for i in range(2 * NU):
                    if i + 1 < 2 * NU:
                        split(i + 1)
                    m = i % NU
                    if m in (1, 2):
                        continue
                    if m >= 3:
                        act.wait_ge(gate_free, q * 4 + (i // NU * 2 + m - 2))
                    for x, (a, w) in enumerate(CHUNKS):
                        act.wait_ge(z_ready, q * (2 * NU * NC) + (NC * i + x + 1 + 2 * NC))
                        src = ps[:, (i % 2) * NC + x, :w]
                        if m == 0:
                            act.activation(ci[:, a:a + w], src, ACT.Copy).then_inc(z_act, 1)
                        else:
                            act.activation(gate[:, m - 3, a:a + w], src, ACT.Sigmoid).then_inc(z_act, 1)
            act.wait_ge(last_ready, 1)
            for x in range(2):
                act.activation(urows[:, x * 512:(x + 1) * 512], ps[:2 + NST, 6 + x], ACT.Copy).then_inc(last_done, 1)

        @block.vector
        def _(dve):
            dve.sem_inc(w_lo, 2)
            dve.memset(up[:, 0:2], 0.0)
            dve.wait_ge(cs_done, 1)
            with dve.Fori(0, KD // 2) as q:
                def split(i):
                    dve.wait_ge(w_hi, q * (2 * NU) + (i + 1))
                    dve.tensor_tensor(wl[:, i % 2], raw[:, i % 2], wh[:, i % 2].bitcast(F32), ALU.subtract).then_inc(w_lo, 1)

                split(0)
                for i in range(2 * NU):
                    if i + 1 < 2 * NU:
                        split(i + 1)
                    m, jj = i % NU, i // NU
                    j = q * 2 + jj
                    if m == 1:
                        dve.tensor_copy(csj[:], cs[:, bass.ds(j, 1)].rearrange("p o s -> p (o s)"))
                        dve.drain()
                        dve.tensor_copy(us[:, :, 0:2], csj[:, :NST].rearrange("p (b t) -> p b t", t=2))
                        dve.wait_ge(z_act, q * (2 * AJ) + (jj * AJ + NC + AJ))
                        for x, (a, w) in enumerate(CHUNKS):
                            dve.wait_ge(z_ready, q * (2 * NU * NC) + (NC * i + x + 1 + 2 * NC))
                            src = ps[:, (i % 2) * NC + x]
                            w0 = min(w, SEQ - a)
                            o = dve.tensor_tensor(up[:, 2 + a:2 + a + w0], src[:, :w0], ci[:, a:a + w0], ALU.mult)
                            if w0 < w:
                                o = dve.tensor_tensor(us[:, :, 2:], src[:, w0:w].rearrange("p (b t) -> p b t", b=DB),
                                                      ci[:, SEQ:].rearrange("p (b t) -> p b t", b=DB), ALU.mult)
                            o.then_inc(z_dve, 1)
                        dve.drain()
                        zs = z[:, SEQ:].rearrange("p (b t) -> p b t", b=DB)
                        tap = [csj[:, NST + x:NST + x + 1] for x in range(3)]
                        dve.tensor_scalar(z[:, :SEQ], up[:, 0:SEQ], tap[0], None, ALU.mult)
                        dve.tensor_scalar(zs, us[:, :, 0:DS], tap[0], None, ALU.mult)
                        for x in (1, 2):
                            dve.drain()
                            dve.scalar_tensor_tensor(out=z[:, :SEQ], in0=up[:, x:x + SEQ], scalar=tap[x],
                                                     in1=z[:, :SEQ], op0=ALU.mult, op1=ALU.add)
                            dve.scalar_tensor_tensor(out=zs, in0=us[:, :, x:x + DS], scalar=tap[x], in1=zs,
                                                     op0=ALU.mult, op1=ALU.add)
                        dve.tensor_copy(ulast[:, bass.ds(j, 1), 0:2], up[:, SEQ:].unsqueeze(1))
                        dve.tensor_copy(ulast[:, bass.ds(j, 1), 2:].rearrange("p o (b t) -> p (o b) t", t=2), us[:, :, DS:])
                        dve.drain()
                    if m == 2:
                        for x, (a, w) in enumerate(CHUNKS):
                            dve.wait_ge(z_ready, q * (2 * NU * NC) + (NC * i + x + 1 + 2 * NC))
                            dve.tensor_tensor(z[:, a:a + w], ps[:, (i % 2) * NC + x, :w], z[:, a:a + w],
                                              ALU.mult).then_inc(z_dve, 1)
                        dve.drain()
                        dve.tensor_copy(k["cvh"][:, bass.ds(j, 1)], z[:].unsqueeze(1))
                        dve.drain()
                        dve.tensor_tensor(k["cvl"][:, bass.ds(j, 1)], z[:].unsqueeze(1),
                                          k["cvh"][:, bass.ds(j, 1)].bitcast(F32), ALU.subtract).then_inc(j_done, 1)
                        dve.drain()

        @block.tensor
        def _(pe):
            pe.sem_inc(z_ready, 2 * NC)
            pe.wait_ge(rows_in, 32)
            for j in range(KD):
                m = pe.transpose(ps[:, 7, j * CS:(j + 1) * CS], rows[:, j * P:(j + 1) * P], k["ident"][:CS, :CS])
            m.then_inc(cs_ready, 1)
            with pe.Fori(0, KD // 2) as q:
                for i in range(2 * NU):
                    m, jj = i % NU, i // NU
                    pe.wait_ge(w_lo, q * (2 * NU) + (i + 3))
                    for x, (a, w) in enumerate(CHUNKS):
                        if m < 3:
                            pe.wait_ge(z_act, q * (2 * AJ) + (jj * AJ + (NC, 2 * NC, AJ)[m] + x + 1))
                        else:
                            pe.wait_ge(z_dve, q * (2 * DJ) + (jj * DJ + (m - 3) * NC + x + 1))
                        for kk in range(KD):
                            o = split3(pe, ps[:, (i % 2) * NC + x, :w], wh[:, i % 2, kk], wl[:, i % 2, kk],
                                       k["xTh"][:, kk, a:a + w], k["xTl"][:, kk, a:a + w], kk == 0, kk == KD - 1)
                        o.then_inc(z_ready, 1)
            pe.wait_ge(j_done, KD)
            pe.wait_ge(cs_done, 1)
            for j in range(KD):
                m = pe.transpose(ps[:2 + NST, 6 + j // 4, (j % 4) * P:(j % 4 + 1) * P], ulast[:, j], k["ident"][:])
            m.then_inc(last_ready, 1)


def branches(nc, io, k):
    KW = SP + KD
    NC = len(CHUNKS)
    with ExitStack() as c:
        def sb(n, s, d=F32):
            return c.enter_context(nc.sbuf_tensor(n, s, d))

        def sem(n):
            return nc.alloc_semaphore(n)

        raw = sb("r_raw", [P, KW, P])
        wh, wl = sb("r_wh", [P, 2, KW, P], F32R), sb("r_wl", [P, 2, KW, P], F32R)
        gate = sb("r_gate", [P, 2, 2, T])
        tc = sb("r_tc", [P, NC, 384])
        mg = sb("r_mg", [P, 2, T])
        atth, attl = k["xTh"], k["xTl"]
        ps = c.enter_context(nc.psum_tensor("r_ps", [P, 8, 512], F32))

        att_in, att_hi, att_lo = sem("r_att_in"), sem("r_att_hi"), sem("r_att_lo")
        raw_in, w_hi, w_lo = sem("r_raw_in"), sem("r_w_hi"), sem("r_w_lo")
        br_ready = sem("br_ready")
        br_done = sem("br_done")
        gate_in = [sem(f"r_gate_in{x}") for x in range(2)]
        mg_out = sem("mg_out")
        mg_free = sem("mg_free")
        block = c.enter_context(nc.Block())
        wa = io["w_branch_attn"][0].rearrange("(k p) (j c) -> j p k c", p=P, c=P)
        wc = io["w_branch_conv"][0].rearrange("(k p) (j c) -> j p k c", p=P, c=P)

        @block.sync
        def _(sp):
            for s in range(SP):
                sp.dma_start(gate[:, s // 2, s % 2], io["s_att"][s]).then_inc(att_in, 16)
            with sp.Fori(0, KD) as j:
                sp.wait_ge(w_lo, j + 1)
                sp.dma_start(raw[:, :SP], wa[j]).then_inc(raw_in, 16)
                sp.dma_start(raw[:, SP:], wc[j]).then_inc(raw_in, 16)

        @block.gpsimd
        def _(pool):
            pool.wait_ge(att_lo, SP)
            with pool.Fori(0, KD // 2) as q:
                for x in range(2):
                    j = q * 2 + x
                    pool.wait_ge(br_done, j * NC + NC)
                    pool.dma_start(gate[:, x], io["s_gate"].rearrange("a j p n -> j p a n")[j]).then_inc(gate_in[x], 16)

        @block.scalar
        def _(act):
            act.sem_inc(mg_free, 2)
            act.wait_ge(att_in, 16 * SP)
            for s in range(SP):
                act.activation(atth[:, s], gate[:, s // 2, s % 2], ACT.Copy).then_inc(att_hi, 1)

            def split(j, x):
                act.wait_ge(raw_in, (j + 1) * 32)
                act.wait_ge(br_ready, j * NC + NC)
                act.activation(wh[:, x], raw[:], ACT.Copy).then_inc(w_hi, 1)

            split(0, 0)
            with act.Fori(0, (KD - 2) // 2) as q:
                for x in range(2):
                    split(q * 2 + (x + 1), 1 - x)
                    act.wait_ge(br_done, (q * 2 + x) * NC + 3 * NC)
                    act.dma_start(io["s_merged"][q * 2 + x], mg[:, x]).then_inc(mg_out, 16)
                    act.wait_ge(mg_out, (q * 2 + x) * 16 + 16)
                    act.sem_inc(mg_free, 1)
            split(KD - 1, 1)
            for j in (KD - 2, KD - 1):
                act.wait_ge(br_done, (j + 3) * NC)
                act.dma_start(io["s_merged"][j], mg[:, j % 2]).then_inc(mg_out, 16)
                act.wait_ge(mg_out, (j + 1) * 16)

        @block.vector
        def _(dve):
            dve.sem_inc(w_lo, 1)
            dve.sem_inc(br_done, 2 * NC)
            for s in range(SP):
                dve.wait_ge(att_hi, s + 1)
                dve.tensor_tensor(attl[:, s], gate[:, s // 2, s % 2], atth[:, s].bitcast(F32),
                                  ALU.subtract).then_inc(att_lo, 1)

            def split(j, x):
                dve.wait_ge(w_hi, j + 1)
                dve.tensor_tensor(wl[:, x], raw[:], wh[:, x].bitcast(F32), ALU.subtract).then_inc(w_lo, 1)

            def merge(j, x, turn):
                dve.wait_ge(gate_in[x], (turn + 1) * 16)
                dve.wait_ge(mg_free, j + 1)
                for y, (a, w) in enumerate(CHUNKS):
                    dve.wait_ge(br_ready, j * NC + (y + 1 + 2 * NC))
                    dve.tensor_tensor(mg[:, x, a:a + w], ps[:, y, :w], gate[:, x, 0, a:a + w], ALU.mult)
                    dve.tensor_tensor(tc[:, y, :w], ps[:, NC + y, :w], gate[:, x, 1, a:a + w], ALU.mult)
                    dve.drain()
                    dve.tensor_tensor(mg[:, x, a:a + w], mg[:, x, a:a + w], tc[:, y, :w], ALU.add).then_inc(br_done, 1)

            split(0, 0)
            with dve.Fori(0, (KD - 2) // 2) as q:
                for x in range(2):
                    split(q * 2 + (x + 1), 1 - x)
                    merge(q * 2 + x, x, q)
            split(KD - 1, 1)
            for j in (KD - 2, KD - 1):
                merge(j, j % 2, j // 2)

        @block.tensor
        def _(pe):
            pe.sem_inc(br_ready, 2 * NC)
            pe.wait_ge(att_lo, SP)
            with pe.Fori(0, KD // 2) as q:
                for x in range(2):
                    j = q * 2 + x
                    pe.wait_ge(w_lo, j + 2)
                    for y, (a, w) in enumerate(CHUNKS):
                        pe.wait_ge(br_done, j * NC + (y + 1 + NC))
                        for kk in range(SP):
                            split3(pe, ps[:, y, :w], wh[:, x, kk], wl[:, x, kk], atth[:, kk, a:a + w],
                                   attl[:, kk, a:a + w], kk == 0, kk == SP - 1)
                        for kk in range(KD):
                            o = split3(pe, ps[:, NC + y, :w], wh[:, x, SP + kk], wl[:, x, SP + kk],
                                       k["cvh"][:, kk, a:a + w], k["cvl"][:, kk, a:a + w], kk == 0, kk == KD - 1)
                        o.then_inc(br_ready, 1)


def over_tiles(eng, step):
    step(0, 0, P)
    with eng.Fori(0, (NT - 3) // 2) as q:
        step(q * 2 + 1, 1, P)
        step(q * 2 + 2, 0, P)
    step(NT - 2, (NT - 2) % 2, P)
    step(NT - 1, (NT - 1) % 2, NS)


class Norm:

    def __init__(self, nc, c, name, gain, bias):
        def sb(n, s):
            return c.enter_context(nc.sbuf_tensor(f"{name}_{n}", s, F32))

        def sem(n):
            return nc.alloc_semaphore(f"{name}_{n}")

        self.gain_src, self.bias_src = gain, bias
        self.res, self.y = sb("res", [P, 2, D]), sb("y", [P, 2, D])
        self.gain, self.bias, self.eps = sb("gain", [P, D]), sb("bias", [P, D]), sb("eps", [P, 1])
        self.st, self.mv = sb("st", [P, 2, 12]), sb("mv", [P, 2, 2])
        self.std, self.rstd = sb("std", [P, 2]), sb("rstd", [P, 2])
        self.consts, self.eps_ready = sem("consts"), sem("eps_ready")
        self.summed = sem("summed")
        self.var_ready, self.std_ready = sem("var_ready"), sem("std_ready")
        self.scaled, self.ready = sem("scaled"), sem("ready")

    def load(self, sp):
        sp.dma_start(self.gain[:], self.gain_src.to_broadcast([P, D])).then_inc(self.consts, 16)
        sp.dma_start(self.bias[:], self.bias_src.to_broadcast([P, D])).then_inc(self.consts, 16)

    def start(self, dve):
        dve.sem_inc(self.summed, 2)
        dve.memset(self.eps[:], EPS).then_inc(self.eps_ready, 1)

    def stats(self, dve, x, n, update):
        y = self.y[:n, x]
        dve.scalar_tensor_tensor(out=y, in0=self.res[:n, x], scalar=ALPHA, in1=update, op0=ALU.mult,
                                 op1=ALU.add).then_inc(self.summed, 1)
        dve.drain()
        for a in range(2):
            dve.bn_stats(self.st[:n, x, 6 * a:6 * a + 6], y[:, 512 * a:512 * (a + 1)])
        dve.drain()
        dve.bn_aggr(self.mv[:n, x], self.st[:n, x]).then_inc(self.var_ready, 1)

    def root(self, act, t, x, n):
        act.wait_ge(self.var_ready, t + 1)
        act.activation(self.std[:n, x:x + 1], self.mv[:n, x, 1:2], ACT.Sqrt, bias=self.eps[:n]).then_inc(self.std_ready, 1)

    def scale(self, dve, t, x, n):
        dve.wait_ge(self.std_ready, t + 1)
        dve.reciprocal(self.rstd[:n, x:x + 1], self.std[:n, x:x + 1])
        dve.drain()
        dve.tensor_scalar(self.y[:n, x], self.y[:n, x], self.mv[:n, x, 0:1], self.rstd[:n, x:x + 1],
                          ALU.subtract, ALU.mult).then_inc(self.scaled, 1)

    def affine(self, pool, t, x, n):
        pool.wait_ge(self.scaled, t + 1)
        pool.tensor_tensor(self.y[:n, x], self.y[:n, x], self.gain[:n], ALU.mult)
        pool.drain()
        pool.tensor_tensor(self.y[:n, x], self.y[:n, x], self.bias[:n], ALU.add).then_inc(self.ready, 1)


def mix_ln1(nc, io, k):
    with ExitStack() as c:
        def sb(n, s, d=F32):
            return c.enter_context(nc.sbuf_tensor(n, s, d))

        def sem(n):
            return nc.alloc_semaphore(n)

        N = Norm(nc, c, "n1", io["ln1_g"], io["ln1_b"])
        wraw = sb("o_raw", [P, 2, D])
        wh, wl = sb("o_wh", [P, KD, D], F32R), sb("o_wl", [P, KD, D], F32R)
        raw = sb("m_raw", [P, 2, KD, P])
        mh, ml = sb("m_h", [P, 2, KD, P], F32R), sb("m_l", [P, 2, KD, P], F32R)
        ps = c.enter_context(nc.psum_tensor("m_ps", [P, 2, 2, D], F32))
        wraw_in = [sem(f"o_raw_in{x}") for x in range(2)]
        w_hi, w_lo = sem("o_w_hi"), sem("o_w_lo")
        tile_in = [sem(f"m_in{x}") for x in range(2)]
        m_hi, m_lo = sem("m_hi"), sem("m_lo")
        y_ready = sem("y_ready")
        h_turned, ht_hi, ht_lo = sem("h_turned"), sem("ht_hi"), sem("ht_lo")
        h_out = [sem(f"h_out{x}") for x in range(2)]
        h_stored = sem("h_stored")
        block = c.enter_context(nc.Block())
        merged = io["s_merged"].rearrange("k p n -> p k n")

        def xrows(t, n):
            if n == P:
                return io["x_prompt"][0].rearrange("(t p) d -> t p d", p=P)[t]
            return io["x_sample"].rearrange("b s d -> (b s) d")

        @block.sync
        def _(sp):
            N.load(sp)
            for kk in range(KD):
                if kk >= 2:
                    sp.wait_ge(w_lo, kk - 1)
                sp.dma_start(wraw[:, kk % 2], io["w_out"][0, kk * P:(kk + 1) * P]).then_inc(wraw_in[kk % 2], 16)

            def step(t, x, n):
                sp.wait_ge(m_lo, t + 1)
                sp.dma_start(raw[:, x, :, :n], merged[:, :, bass.ds(t * P, n)]).then_inc(tile_in[x], 16)
                sp.wait_ge(N.summed, t + 1)
                sp.dma_start(N.res[:n, x], xrows(t, n)).then_inc(tile_in[x], 16)
            over_tiles(sp, step)

        @block.scalar
        def _(act):
            for kk in range(KD):
                act.wait_ge(wraw_in[kk % 2], 16 * (kk // 2 + 1))
                act.activation(wh[:, kk], wraw[:, kk % 2], ACT.Copy).then_inc(w_hi, 1)
            act.wait_ge(N.eps_ready, 1)

            def turned(t, x, n):
                act.wait_ge(h_turned, t + 1)
                act.activation(k["hTh"][:, :, bass.ds(t * P, n)],
                               ps[:, 1, x].rearrange("p (j n) -> p j n", j=KD)[:, :, :n], ACT.Copy).then_inc(ht_hi, 1)

            def step(t, x, n):
                act.wait_ge(tile_in[x], (t - x) * 16 + 32)
                act.wait_ge(y_ready, t + 1)
                act.activation(mh[:, x, :, :n], raw[:, x, :, :n], ACT.Copy).then_inc(m_hi, 1)
                if not isinstance(t, int) or t:
                    turned(t - 1, 1 - x, P)
                N.root(act, t, x, n)
            over_tiles(act, step)
            turned(NT - 1, (NT - 1) % 2, NS)

        @block.vector
        def _(dve):
            N.start(dve)
            dve.sem_inc(m_lo, 2)
            dve.sem_inc(ht_lo, 2)
            for kk in range(KD):
                dve.wait_ge(w_hi, kk + 1)
                dve.tensor_tensor(wl[:, kk], wraw[:, kk % 2], wh[:, kk].bitcast(F32), ALU.subtract).then_inc(w_lo, 1)

            def turned(t, x, n):
                dve.wait_ge(ht_hi, t + 1)
                at = bass.ds(t * P, n)
                dve.tensor_tensor(k["hTl"][:, :, at], ps[:, 1, x].rearrange("p (j n) -> p j n", j=KD)[:, :, :n],
                                  k["hTh"][:, :, at].bitcast(F32), ALU.subtract).then_inc(ht_lo, 1)

            def step(t, x, n):
                dve.wait_ge(m_hi, t + 1)
                dve.tensor_tensor(ml[:, x, :, :n], raw[:, x, :, :n], mh[:, x, :, :n].bitcast(F32),
                                  ALU.subtract).then_inc(m_lo, 1)
                if not isinstance(t, int) or t:
                    turned(t - 1, 1 - x, P)
                dve.wait_ge(h_stored, t + 1)
                dve.wait_ge(y_ready, t + 3)
                N.stats(dve, x, n, ps[:n, 0, x])
                N.scale(dve, t, x, n)
            over_tiles(dve, step)
            turned(NT - 1, (NT - 1) % 2, NS)

        @block.gpsimd
        def _(pool):
            pool.sem_inc(h_stored, 2)
            pool.wait_ge(N.consts, 32)

            def step(t, x, n):
                N.affine(pool, t, x, n)
                pool.wait_ge(N.ready, t + 1)
                pool.dma_start(io["s_h"][bass.ds(t * P, n)], N.y[:n, x]).then_inc(h_out[x], 16)
                pool.wait_ge(h_out[x], (t - x) * 8 + 16)
                pool.sem_inc(h_stored, 1)
            over_tiles(pool, step)

        @block.tensor
        def _(pe):
            pe.sem_inc(y_ready, 2)
            pe.wait_ge(w_lo, KD)

            def turn(t, x, n):
                pe.wait_ge(N.ready, t + 1)
                pe.wait_ge(ht_lo, t + 1)
                for j in range(KD):
                    m = pe.transpose(ps[:, 1, x, j * P:j * P + n], N.y[:n, x, j * P:(j + 1) * P], k["ident"][:n, :n])
                m.then_inc(h_turned, 1)

            def step(t, x, n):
                pe.wait_ge(m_lo, t + 3)
                pe.wait_ge(N.summed, t + 1)
                for a in range(2):
                    for kk in range(KD):
                        m = split3(pe, ps[:n, 0, x, a * 512:(a + 1) * 512], mh[:, x, kk, :n], ml[:, x, kk, :n],
                                   wh[:, kk, a * 512:(a + 1) * 512], wl[:, kk, a * 512:(a + 1) * 512],
                                   kk == 0, kk == KD - 1)
                m.then_inc(y_ready, 1)
                if not isinstance(t, int) or t:
                    turn(t - 1, 1 - x, P)
            over_tiles(pe, step)
            turn(NT - 1, (NT - 1) % 2, NS)


def retrieve(nc, io, k):
    K = TOPK
    NC = len(CHUNKS)
    NU = 2 * HEADS
    with ExitStack() as c:
        def sb(n, s, d=F32):
            return c.enter_context(nc.sbuf_tensor(n, s, d))

        def sem(n):
            return nc.alloc_semaphore(n)

        raw = sb("q_raw", [P, 2, KD, P])
        wh, wl = sb("q_wh", [P, 2, KD, P], F32R), sb("q_wl", [P, 2, KD, P], F32R)
        keys = sb("keys", [P, 2, P])
        kh, kl = sb("keys_h", [P, 2, P], F32R), sb("keys_l", [P, 2, P], F32R)
        qh, ql = sb("q_h", [P, 2, T], F32R), sb("q_l", [P, 2, T], F32R)
        s1 = sb("scores", [P, 2, 2, NT, P])
        wk = sb("scores_rest", [P, 2, NT, P])
        v, ix, ixf = sb("top_v", [P, 2, NT, K]), sb("top_i", [P, 2, NT, K], U32), sb("top_if", [P, 2, NT, K])
        cand, rest = sb("cand", [P, NT, K, K]), sb("cand_rest", [P, NT, K * K])
        sc, pos = sb("best", [P, NT, K]), sb("best_pos", [P, NT, K], U32)
        hl, hlf = sb("pos_parts", [P, 2, NT, K], U32), sb("pos_parts_f", [P, 2, NT, K])
        ex, tot, rtot = sb("ex", [P, NT, K]), sb("tot", [P, NT]), sb("rtot", [P, NT])
        count, tick = sb("count16", [P, K]), sb("q_tick", [P, 1])
        sel = k["sel"]
        ps = c.enter_context(nc.psum_tensor("q_ps", [P, 8, 512], F32))

        consts = sem("q_consts")
        keys_turned, keys_hi, keys_lo = sem("keys_turned"), sem("keys_hi"), sem("keys_lo")
        raw_in = [sem(f"q_raw_in{x}") for x in range(2)]
        w_hi, w_lo = sem("q_w_hi"), sem("q_w_lo")
        q_ready = sem("q_ready")
        q_hi, q_lo = sem("q_hi"), sem("q_lo")
        s_ready = sem("q_s_ready")
        s_copied = sem("q_s_copied")
        topped = sem("topped")
        e_ready, e_done = sem("e_ready"), sem("e_done")
        block = c.enter_context(nc.Block())
        w_view = io["peer_w_q"][0].rearrange("(k p) (h x c) -> x h p k c", p=P, x=2, c=P)

        @block.sync
        def _(sp):
            sp.dma_start(keys[:, 0], io["peer_keys_1"][0]).then_inc(consts, 16)
            sp.dma_start(keys[:, 1], io["peer_keys_2"][0]).then_inc(consts, 16)
            sp.dma_start(count[:], io["c_count"][:, :K]).then_inc(consts, 16)
            with sp.Fori(0, HEADS) as h:
                for x in range(2):
                    sp.wait_ge(w_lo, h * 2 + (x + 1))
                    sp.dma_start(raw[:, x], w_view[x, h]).then_inc(raw_in[x], 16)

        @block.scalar
        def _(act):
            act.sem_inc(s_copied, 1)
            act.wait_ge(keys_turned, 1)
            act.activation(kh[:], ps[:, 7, :2 * P].rearrange("p (x n) -> p x n", x=2), ACT.Copy).then_inc(keys_hi, 1)

            def queries(h):
                for x in range(2):
                    act.wait_ge(raw_in[x], (h + 1) * 16)
                    act.wait_ge(q_ready, h * (2 * NC) + ((x + 1) * NC))
                    act.activation(wh[:, x], raw[:, x], ACT.Copy).then_inc(w_hi, 1)
                for x in range(2):
                    for y, (a, w) in enumerate(CHUNKS):
                        act.wait_ge(q_ready, h * (2 * NC) + (x * NC + y + 1 + 2 * NC))
                        act.wait_ge(s_ready, h * 2 + (x + 1))
                        act.activation(qh[:, x, a:a + w], ps[:, y, :w], ACT.Copy).then_inc(q_hi, 1)

            def scores(h, p):
                act.wait_ge(topped, h + 1)
                for x in range(2):
                    act.wait_ge(s_ready, h * 2 + (x + 3))
                    act.activation(s1[:, p, x, :PT], ps[:, 3:5].rearrange("p b (t n) -> p (b t) n", n=P), ACT.Copy)
                    act.activation(s1[:NS, p, x, PT], ps[:NS, 5, :P], ACT.Copy).then_inc(s_copied, 1)

            def exp(h):
                act.wait_ge(e_ready, h + 1)
                act.activation(ex[:], ex[:], ACT.Exp).then_inc(e_done, 1)

            queries(0)
            scores(0, 0)
            with act.Fori(0, (HEADS - 2) // 2) as q:
                for p in range(2):
                    queries(q * 2 + (p + 1))
                    scores(q * 2 + (p + 1), 1 - p)
                    exp(q * 2 + p)
            queries(HEADS - 1)
            scores(HEADS - 1, 1)
            exp(HEADS - 2)
            exp(HEADS - 1)

        @block.gpsimd
        def _(pool):
            pool.sem_inc(w_lo, 2)
            with pool.Fori(0, HEADS) as h:
                for x in range(2):
                    pool.wait_ge(w_hi, h * 2 + (x + 1))
                    pool.tensor_tensor(wl[:, x], raw[:, x], wh[:, x].bitcast(F32), ALU.subtract).then_inc(w_lo, 1)

        @block.vector
        def _(dve):
            dve.sem_inc(q_lo, NC)
            dve.sem_inc(topped, 2)
            for b in (v, ix, sc, pos):
                dve.memset(b[:], 0)
            dve.wait_ge(keys_hi, 1)
            dve.tensor_tensor(kl[:], ps[:, 7, :2 * P].rearrange("p (x n) -> p x n", x=2), kh[:].bitcast(F32),
                              ALU.subtract).then_inc(keys_lo, 1)
            dve.wait_ge(consts, 48)

            def queries(h):
                for x in range(2):
                    for y, (a, w) in enumerate(CHUNKS):
                        dve.wait_ge(q_hi, h * (2 * NC) + (x * NC + y + 1))
                        dve.tensor_tensor(ql[:, x, a:a + w], ps[:, y, :w], qh[:, x, a:a + w].bitcast(F32),
                                          ALU.subtract).then_inc(q_lo, 1)

            def top16(vals, spare, out_v, out_i):
                def each(f):
                    for t in range(NT):
                        f(t, rows_of(t))
                    dve.drain()
                each(lambda t, n: dve.max(out_v(t, n, 0), vals(t, n)))
                each(lambda t, n: dve.match_replace(spare(t, n), out_v(t, n, 0), vals(t, n), LOW))
                each(lambda t, n: dve.max(out_v(t, n, 8), spare(t, n)))
                each(lambda t, n: dve.max_index(out_i(t, n, 0), out_v(t, n, 0), vals(t, n)))
                each(lambda t, n: dve.max_index(out_i(t, n, 8), out_v(t, n, 8), spare(t, n)))

            def top(h, p):
                dve.wait_ge(s_copied, h * 2 + 3)
                dve.memset(tick[:], 0.0)
                for x in range(2):
                    top16(lambda t, n: s1[:n, p, x, t], lambda t, n: wk[:n, x, t],
                          lambda t, n, a: v[:n, x, t, a:a + 8], lambda t, n, a: ix[:n, x, t, a:a + 8])
                dve.tensor_tensor(cand[:], v[:, 0].unsqueeze(3).to_broadcast([P, NT, K, K]),
                                  v[:, 1].unsqueeze(2).to_broadcast([P, NT, K, K]), ALU.add).then_inc(topped, 1)
                dve.tensor_copy(ixf[:], ix[:])
                dve.drain()
                top16(lambda t, n: cand[:n, t].rearrange("p a b -> p (a b)"), lambda t, n: rest[:n, t],
                      lambda t, n, a: sc[:n, t, a:a + 8], lambda t, n, a: pos[:n, t, a:a + 8])
                dve.tensor_tensor(ex[:], sc[:], sc[:, :, 0:1].to_broadcast([P, NT, K]), ALU.subtract).then_inc(e_ready, 1)
                dve.tensor_scalar(hl[:, 0], pos[:], 4, None, ALU.logical_shift_right)
                dve.tensor_scalar(hl[:, 1], pos[:], K - 1, None, ALU.bitwise_and)
                dve.drain()
                dve.tensor_copy(hlf[:], hl[:])
                dve.drain()
                hot = cand
                for x in range(2):
                    dve.tensor_tensor(hot[:], hlf[:, x].unsqueeze(3).to_broadcast([P, NT, K, K]),
                                      count[:].unsqueeze(1).unsqueeze(1).to_broadcast([P, NT, K, K]), ALU.is_equal)
                    dve.drain()
                    dve.tensor_tensor(hot[:], hot[:], ixf[:, x].unsqueeze(2).to_broadcast([P, NT, K, K]), ALU.mult)
                    dve.drain()
                    dve.tensor_reduce(sel[:, x, :, bass.ds(h * K, K)], hot[:], AX.X, ALU.add)
                    dve.drain()
                dve.wait_ge(e_done, h + 1)
                dve.tensor_reduce(tot[:], ex[:], AX.X, ALU.add)
                dve.drain()
                dve.reciprocal(rtot[:], tot[:])
                dve.drain()
                dve.tensor_tensor(sel[:, 2, :, bass.ds(h * K, K)], ex[:],
                                  rtot[:].unsqueeze(2).to_broadcast([P, NT, K]), ALU.mult)
                dve.drain()

            queries(0)
            with dve.Fori(0, (HEADS - 2) // 2) as q:
                for p in range(2):
                    queries(q * 2 + (p + 1))
                    top(q * 2 + p, p)
            queries(HEADS - 1)
            top(HEADS - 2, 0)
            top(HEADS - 1, 1)

        @block.tensor
        def _(pe):
            pe.sem_inc(q_ready, 2 * NC)
            pe.sem_inc(s_ready, 2)
            pe.wait_ge(consts, 48)
            for x in range(2):
                m = pe.transpose(ps[:, 7, x * P:(x + 1) * P], keys[:, x], k["ident"][:])
            m.then_inc(keys_turned, 1)
            pe.wait_ge(keys_lo, 1)
            with pe.Fori(0, HEADS) as h:
                for x in range(2):
                    pe.wait_ge(w_lo, h * 2 + (x + 3))
                    for y, (a, w) in enumerate(CHUNKS):
                        pe.wait_ge(q_lo, h * (2 * NC) + (x * NC + y + 1))
                        for kk in range(KD):
                            m = split3(pe, ps[:, y, :w], wh[:, x, kk], wl[:, x, kk], k["hTh"][:, kk, a:a + w],
                                       k["hTl"][:, kk, a:a + w], kk == 0, kk == KD - 1)
                        m.then_inc(q_ready, 1)
                for x in range(2):
                    pe.wait_ge(q_lo, h * (2 * NC) + ((x + 2) * NC))
                    pe.wait_ge(s_copied, h * 2 + (x + 1))
                    for t in range(NT):
                        n = rows_of(t)
                        m = split3(pe, ps[:n, 3 + t // 4, (t % 4) * P:(t % 4 + 1) * P], qh[:, x, t * P:t * P + n],
                                   ql[:, x, t * P:t * P + n], kh[:, x], kl[:, x], True, True)
                    m.then_inc(s_ready, 1)


GB = 64
GT = 4


def build_gates(nc, io, k):
    NB = T // GB
    NGR = GB // GT
    RB = 4
    with ExitStack() as c:
        def sb(n, s, d=F32):
            return c.enter_context(nc.sbuf_tensor(n, s, d))

        def sem(n):
            return nc.alloc_semaphore(n)

        sel = k["sel"]
        selT = sb("selT", [P, 3, T])
        count = sb("count", [P, P])
        hot = sb("hot", [P, RB, 2, GT, P])
        blk = sb("gate_block", [P, 2, P, GB])
        ps = c.enter_context(nc.psum_tensor("g_ps", [P, 8, 512], F32))
        count_in, t_ready, t_done = sem("count_in"), sem("sel_turned"), sem("sel_copied")
        hot_ready, hot_weighed = sem("hot_ready"), sem("hot_weighed")
        g_ready = sem("g_ready")
        g_done = sem("g_done")
        blk_out = [sem(f"blk_out{x}") for x in range(2)]
        blk_free = sem("blk_free")
        block = c.enter_context(nc.Block())

        def over_blocks(eng, step):
            with eng.Fori(0, NB // 2) as q:
                step(q * 2, 0)
                step(q * 2 + 1, 1)
            step(NB - 1, 0)

        @block.sync
        def _(sp):
            sp.dma_start(count[:], io["c_count"]).then_inc(count_in, 16)
            sp.sem_inc(blk_free, 2)

            def step(b, x):
                sp.wait_ge(g_done, b * NGR + (NGR + RB))
                sp.dma_start(io["s_g"][b].rearrange("p i t -> p (i t)"), blk[:, x].rearrange("p i t -> p (i t)")).then_inc(blk_out[x], 16)
                sp.wait_ge(blk_out[x], (b - x) * 8 + 16)
                sp.sem_inc(blk_free, 1)
            over_blocks(sp, step)

        @block.scalar
        def _(act):
            act.sem_inc(g_done, RB)
            for t in range(NT):
                n = rows_of(t)
                act.wait_ge(t_ready, t + 1)
                act.activation(selT[:, :, t * P:t * P + n], ps[:, 4 + t % 2, :3 * P].rearrange("p (w n) -> p w n", w=3)[:, :, :n],
                               ACT.Copy).then_inc(t_done, 1)

            def step(b, x):
                for g in range(NGR):
                    if g == 0:
                        act.wait_ge(blk_free, b + 1)
                    act.wait_ge(g_ready, b * NGR + (g + 1 + RB))
                    act.activation(blk[:, x, :, g * GT:(g + 1) * GT].rearrange("p i t -> p t i"),
                                   ps[:, g % RB].rearrange("p (t i) -> p t i", t=GT), ACT.Copy).then_inc(g_done, 1)
            over_blocks(act, step)

        @block.vector
        def _(dve):
            dve.wait_ge(count_in, 16)
            dve.wait_ge(t_done, NT)

            def step(b, x):
                for g in range(NGR):
                    dve.wait_ge(g_ready, b * NGR + (g + 1))
                    dve.tensor_tensor(hot[:, g % RB], count[:].unsqueeze(1).unsqueeze(1).to_broadcast([P, 2, GT, P]),
                                      selT[:, 0:2, bass.ds(b * GB + g * GT, GT)].unsqueeze(3).to_broadcast([P, 2, GT, P]),
                                      ALU.is_equal).then_inc(hot_ready, 1)
            over_blocks(dve, step)

        @block.gpsimd
        def _(pool):
            pool.wait_ge(t_done, NT)

            def step(b, x):
                for g in range(NGR):
                    pool.wait_ge(hot_ready, b * NGR + (g + 1))
                    pool.tensor_tensor(hot[:, g % RB, 1], hot[:, g % RB, 1],
                                       selT[:, 2, bass.ds(b * GB + g * GT, GT)].unsqueeze(2).to_broadcast([P, GT, P]),
                                       ALU.mult).then_inc(hot_weighed, 1)
            over_blocks(pool, step)

        @block.tensor
        def _(pe):
            for t in range(NT):
                n = rows_of(t)
                if t >= 2:
                    pe.wait_ge(t_done, t - 1)
                for w in range(3):
                    m = pe.transpose(ps[:, 4 + t % 2, w * P:w * P + n], sel[:n, w, t], k["ident"][:n, :n])
                m.then_inc(t_ready, 1)
            pe.sem_inc(g_ready, RB)

            def step(b, x):
                for g in range(NGR):
                    pe.wait_ge(hot_weighed, b * NGR + (g + 1))
                    pe.wait_ge(g_done, b * NGR + (g + 1))
                    for y in range(GT):
                        m = pe.matmul(ps[:, g % RB, y * P:(y + 1) * P], hot[:, g % RB, 0, y], hot[:, g % RB, 1, y],
                                      start=True, stop=True)
                    m.then_inc(g_ready, 1)
            over_blocks(pe, step)


def experts(nc, io, k):
    NPAIR = KEYS // 2
    NB = T // GB
    NC = len(CHUNKS)
    HD2 = KD // 2
    with ExitStack() as c:
        def sb(n, s, d=F32):
            return c.enter_context(nc.sbuf_tensor(n, s, d))

        def sem(n):
            return nc.alloc_semaphore(n)

        uraw, vraw = sb("u_raw", [P, 2, D]), sb("v_raw", [P, 2, D])
        uh, ul = sb("u_h", [P, KD, P], F32R), sb("u_l", [P, KD, P], F32R)
        vh, vl = sb("v_h", [P, 2, D], F32R), sb("v_l", [P, 2, D], F32R)
        ch, cl = sb("coef_h", [P, 4, T], F32R), sb("coef_l", [P, 4, T], F32R)
        gate = sb("x_gate", [P, 2, NB, 2, GB])
        tmp = sb("x_tmp", [P, 2, T])
        acc = k["acc"]
        ps = c.enter_context(nc.psum_tensor("e_ps", [P, 8, 512], F32))
        psT = ps[:, 0:2].rearrange("p b n -> p (b n)")

        u_in = [sem(f"u_in{x}") for x in range(2)]
        v_in = [sem(f"v_in{x}") for x in range(2)]
        gate_in = [sem(f"xg_in{x}") for x in range(2)]
        u_turned = sem("u_turned")
        u_hi, u_lo = sem("u_hi"), sem("u_lo")
        a_ready = sem("a_ready")
        gelu_done = sem("gelu_done")
        c_done = sem("c_done")
        v_hi, v_lo = sem("v_hi"), sem("v_lo")
        o_ready = sem("xo_ready")
        o_added = sem("o_added")
        block = c.enter_context(nc.Block())
        u_view = io["peer_u"][0].rearrange("(p i) d -> i p d", i=KEYS)
        v_view = io["peer_v"][0].rearrange("(p i) d -> i p d", i=KEYS)
        g_view = io["s_g"].rearrange("b p (i w) t -> i p b (w t)", w=2)

        def over_pairs(eng, step):
            step(0, 0, False)
            with eng.Fori(0, (NPAIR - 2) // 2) as q:
                step(q * 2 + 1, 1, True)
                step(q * 2 + 2, 0, True)
            step(NPAIR - 1, 1, True)

        @block.sync
        def _(sp):
            def step(p, x, values):
                for w in range(2):
                    sp.wait_ge(u_turned, p * 2 + (w + 1))
                    sp.dma_start(uraw[:, w], u_view[p * 2 + w]).then_inc(u_in[w], 16)
                sp.wait_ge(c_done, p * 2 + 2)
                sp.dma_start(gate[:, x].rearrange("p b w t -> p b (w t)"), g_view[p]).then_inc(gate_in[x], 16)
                for w in range(2):
                    sp.wait_ge(v_lo, p * 2 + (w + 1))
                    sp.dma_start(vraw[:, w], v_view[p * 2 + w]).then_inc(v_in[w], 16)
            over_pairs(sp, step)

        @block.scalar
        def _(act):
            act.sem_inc(gelu_done, NC)

            def split_u(e):
                act.wait_ge(u_turned, e + 3)
                act.wait_ge(a_ready, e * NC + NC)
                act.activation(uh[:], psT.rearrange("p (k n) -> p k n", k=KD), ACT.Copy).then_inc(u_hi, 1)

            def gelu(e, w):
                for y, (a, n) in enumerate(CHUNKS):
                    act.wait_ge(a_ready, e * NC + (y + 1 + NC))
                    if y == 0:
                        act.wait_ge(c_done, e + 3)
                    act.activation(tmp[:, w, a:a + n], ps[:, 2 + y, :n], ACT.Gelu).then_inc(gelu_done, 1)

            def split_v(p):
                act.wait_ge(o_ready, (p + 1) * (KD * NC))
                for w in range(2):
                    act.wait_ge(v_in[w], (p + 1) * 16)
                    act.activation(vh[:, w], vraw[:, w], ACT.Copy).then_inc(v_hi, 1)

            def step(p, x, values):
                for w in range(2):
                    if w == 0 and values:
                        split_v(p - 1)
                    gelu(p * 2 + w, w)
                    if not (isinstance(p, int) and p * 2 + w == KEYS - 1):
                        split_u(p * 2 + w + 1)
            split_u(0)
            over_pairs(act, step)
            split_v(NPAIR - 1)

        @block.gpsimd
        def _(pool):
            pool.sem_inc(c_done, 4)

            def step(p, x, values):
                for w in range(2):
                    e, s = p * 2 + w, 2 * x + w
                    if w == 0:
                        pool.wait_ge(gate_in[x], (p - x) * 8 + 16)
                    pool.wait_ge(gelu_done, e * NC + 2 * NC)
                    if values:
                        pool.wait_ge(o_ready, p * (KD * NC))
                    t3 = tmp[:, w].rearrange("p (b t) -> p b t", t=GB)
                    pool.tensor_tensor(t3, t3, gate[:, x, :, w], ALU.mult)
                    pool.drain()
                    pool.tensor_copy(ch[:, s], tmp[:, w])
                    pool.drain()
                    pool.tensor_tensor(cl[:, s], tmp[:, w], ch[:, s].bitcast(F32), ALU.subtract).then_inc(c_done, 1)
            over_pairs(pool, step)

        @block.vector
        def _(dve):
            dve.memset(acc[:], 0.0)
            dve.sem_inc(u_lo, 1)
            dve.sem_inc(v_lo, 2)
            dve.sem_inc(o_added, NC)

            def split_u(e):
                dve.wait_ge(u_hi, e + 1)
                dve.tensor_tensor(ul[:], psT.rearrange("p (k n) -> p k n", k=KD), uh[:].bitcast(F32),
                                  ALU.subtract).then_inc(u_lo, 1)

            def split_v(p):
                for w in range(2):
                    dve.wait_ge(v_hi, p * 2 + (w + 1))
                    dve.tensor_tensor(vl[:, w], vraw[:, w], vh[:, w].bitcast(F32), ALU.subtract).then_inc(v_lo, 1)

            def add(p, ds):
                for d in ds:
                    for y, (a, n) in enumerate(CHUNKS):
                        dve.wait_ge(o_ready, p * (KD * NC) + (d * NC + y + 1 + KD * NC))
                        dve.tensor_tensor(acc[:, d, a:a + n], ps[:, 5 + y, :n], acc[:, d, a:a + n],
                                          ALU.add).then_inc(o_added, 1)

            def step(p, x, values):
                for w in range(2):
                    d = w * HD2
                    if w == 0 and values:
                        split_v(p - 1)
                    if values:
                        add(p - 1, [d])
                    if not (isinstance(p, int) and p * 2 + w == KEYS - 1):
                        split_u(p * 2 + w + 1)
                    if values:
                        add(p - 1, [d + 1])
                    if values:
                        add(p - 1, [d + 2, d + 3])
            split_u(0)
            over_pairs(dve, step)
            split_v(NPAIR - 1)
            add(NPAIR - 1, range(KD))

        @block.tensor
        def _(pe):
            pe.sem_inc(u_turned, 2)
            pe.sem_inc(a_ready, NC)
            pe.sem_inc(o_ready, KD * NC)

            def turn(e, w, p):
                pe.wait_ge(u_in[w], (p + 1) * 16)
                pe.wait_ge(u_lo, e + 1)
                for j in range(KD):
                    m = pe.transpose(psT[:, j * P:(j + 1) * P], uraw[:, w, j * P:(j + 1) * P], k["ident"][:])
                m.then_inc(u_turned, 1)

            def activations(e):
                pe.wait_ge(u_lo, e + 2)
                for y, (a, n) in enumerate(CHUNKS):
                    pe.wait_ge(gelu_done, e * NC + (y + 1))
                    for kk in range(KD):
                        m = split3(pe, ps[:, 2 + y, :n], uh[:, kk], ul[:, kk], k["hTh"][:, kk, a:a + n],
                                   k["hTl"][:, kk, a:a + n], kk == 0, kk == KD - 1)
                    m.then_inc(a_ready, 1)

            def values(p, x, half):
                if half == 0:
                    pe.wait_ge(v_lo, p * 2 + 4)
                    pe.wait_ge(c_done, p * 2 + 6)
                for d in range(half * HD2, (half + 1) * HD2):
                    for y, (a, n) in enumerate(CHUNKS):
                        pe.wait_ge(o_added, p * (KD * NC) + (d * NC + y + 1))
                        for w in range(2):
                            s = 2 * x + w
                            m = split3(pe, ps[:, 5 + y, :n], vh[:, w, d * P:(d + 1) * P], vl[:, w, d * P:(d + 1) * P],
                                       ch[:, s, a:a + n], cl[:, s, a:a + n], w == 0, w == 1)
                        m.then_inc(o_ready, 1)

            turn(0, 0, 0)

            def step(p, x, vals):
                for w in range(2):
                    e = p * 2 + w
                    activations(e)
                    if w == 0:
                        turn(e + 1, 1, p)
                    elif not (isinstance(p, int) and p == NPAIR - 1):
                        turn(e + 1, 0, p + 1)
                    if vals:
                        values(p - 1, 1 - x, w)
            over_pairs(pe, step)
            values(NPAIR - 1, 1, 0)
            values(NPAIR - 1, 1, 1)


def ln2_out(nc, io, k):
    with ExitStack() as c:
        def sem(n):
            return nc.alloc_semaphore(n)

        N = Norm(nc, c, "n2", io["ln2_g"], io["ln2_b"])
        stage = c.enter_context(nc.sbuf_tensor("f_stage", [P, 2, KD, P], F32))
        ps = c.enter_context(nc.psum_tensor("f_ps", [P, 2, D], F32))
        h_in = [sem(f"h_in{x}") for x in range(2)]
        staged = sem("staged")
        f_ready = sem("f_ready")
        y_out = [sem(f"y_out{x}") for x in range(2)]
        y_stored = sem("y_stored")
        block = c.enter_context(nc.Block())

        @block.sync
        def _(sp):
            N.load(sp)

            def step(t, x, n):
                sp.wait_ge(N.summed, t + 1)
                sp.dma_start(N.res[:n, x], io["s_h"][bass.ds(t * P, n)]).then_inc(h_in[x], 16)
            over_tiles(sp, step)

        @block.scalar
        def _(act):
            act.wait_ge(N.eps_ready, 1)

            def step(t, x, n):
                act.wait_ge(f_ready, t + 1)
                act.activation(stage[:, x, :, :n], k["acc"][:, :, bass.ds(t * P, n)], ACT.Copy).then_inc(staged, 1)
                N.root(act, t, x, n)
            over_tiles(act, step)

        @block.vector
        def _(dve):
            N.start(dve)

            def step(t, x, n):
                dve.wait_ge(y_stored, t + 1)
                dve.wait_ge(h_in[x], (t - x) * 8 + 16)
                dve.wait_ge(f_ready, t + 3)
                N.stats(dve, x, n, ps[:n, x])
                N.scale(dve, t, x, n)
            over_tiles(dve, step)

        @block.gpsimd
        def _(pool):
            pool.sem_inc(y_stored, 2)
            pool.wait_ge(N.consts, 32)

            def step(t, x, n):
                N.affine(pool, t, x, n)
                pool.wait_ge(N.ready, t + 1)
                dst = io["o_y_prompt"][0].rearrange("(t p) d -> t p d", p=P)[t] if n == P else \
                    io["o_y_sample"].rearrange("b s d -> (b s) d")
                pool.dma_start(dst, N.y[:n, x]).then_inc(y_out[x], 16)
                pool.wait_ge(y_out[x], (t - x) * 8 + 16)
                pool.sem_inc(y_stored, 1)
            over_tiles(pool, step)

        @block.tensor
        def _(pe):
            pe.sem_inc(f_ready, 2)

            def step(t, x, n):
                pe.wait_ge(staged, t + 1)
                pe.wait_ge(N.summed, t + 1)
                for j in range(KD):
                    m = pe.transpose(ps[:n, x, j * P:(j + 1) * P], stage[:, x, j, :n], k["ident"][:])
                m.then_inc(f_ready, 1)
            over_tiles(pe, step)


def program(nc, io, phases=99):
    def scratch(name, shape):
        io[name] = nc.dram_tensor(name, shape, F32).ap()

    scratch("s_qkv", (3, NG, DB, DS, AW))
    scratch("s_att", (SP, P, T))
    scratch("s_gate", (2, KD, P, T))
    scratch("s_merged", (KD, P, T))
    scratch("s_h", (T, D))
    scratch("s_g", ((T + GB - 1) // GB, P, KEYS, GB))
    with ExitStack() as c:
        k = {"ident": c.enter_context(nc.sbuf_tensor("ident", [P, P], F32)),
             "cache_moved": c.enter_context(nc.semaphore("cache_moved"))}
        done = 0

        def phase(f, *more):
            nonlocal done
            done += 1
            if done <= phases:
                f(nc, io, k, *more)

        mixer_sems = nc.snapshot_sems()
        with ExitStack() as mixer:
            for n in ("xTh", "xTl"):
                k[n] = mixer.enter_context(nc.sbuf_tensor(n, [P, KD, T], F32R))
            phase(load_x)
            phase(prompt_attn)
            phase(sample_attn)
            with ExitStack() as conv:
                for n in ("cvh", "cvl"):
                    k[n] = conv.enter_context(nc.sbuf_tensor(n, [P, KD, T], F32R))
                phase(conv_gates)
                phase(branches)
        with ExitStack() as peer:
            for n in ("hTh", "hTl"):
                k[n] = peer.enter_context(nc.sbuf_tensor(n, [P, KD, T], F32R))
            phase(mix_ln1)
            nc.clear_and_free_semaphores(nc.allocated_since(mixer_sems))
            nc.all_engine_barrier()
            with ExitStack() as ret:
                k["sel"] = ret.enter_context(nc.sbuf_tensor("sel", [P, 3, NT, P], F32))
                phase(retrieve)
                phase(build_gates)
            k["acc"] = peer.enter_context(nc.sbuf_tensor("acc", [P, KD, T], F32))
            phase(experts)
            phase(ln2_out)
        with nc.Block() as block:
            @block.scalar
            def _(act):
                act.wait_ge(k["cache_moved"], 16 * NG * SP)


_INS = ["x_prompt", "x_sample", "cache_kv_w128", "cache_kv_w512", "cache_kv_w2048", "state_conv", "w_in", "conv_w",
        "w_branch_attn", "w_branch_conv", "w_out", "ln1_g", "ln1_b", "peer_w_q", "peer_keys_1", "peer_keys_2",
        "peer_u", "peer_v", "ln2_g", "ln2_b"]
_OUTS = [("o_y_prompt", (1, SEQ, D)), ("o_y_sample", (DB, DS, D)),
         ("o_kv0_prompt", (1, 1, 128, 2, SLOTS, HD)), ("o_kv1_prompt", (1, 1, 512, 2, SLOTS, HD)),
         ("o_kv2_prompt", (1, 1, 1024, 2, SLOTS, HD)), ("o_conv_prompt", (1, 1, 2, D)),
         ("o_kv0_sample", (1, DB, 128, 2, SLOTS, HD)), ("o_kv1_sample", (1, DB, 512, 2, SLOTS, HD)),
         ("o_kv2_sample", (1, DB, 1024, 2, SLOTS, HD)), ("o_conv_sample", (1, DB, 2, D))]


def shape_constants():
    pos = np.arange(NT * P).astype(np.float32)
    pos[SEQ:T] = SEQ + np.arange(NS) % DS
    pos[T:] = 0
    inv = np.power(np.float32(10000.0), -np.arange(32, dtype=np.float32) / np.float32(32)).astype(np.float32)
    ang = pos[:, None] * inv[None, :]
    cos, sin = np.cos(ang).astype(np.float32), np.sin(ang).astype(np.float32)
    cos = cos.reshape(NT, P, 32).transpose(1, 0, 2)
    sin = np.stack([-sin, sin], 1).reshape(NT, P, 2, 32).transpose(1, 0, 2, 3)
    q = np.arange(P)[:, None]

    def visible(dist, g):
        win, dil = GROUPS[g]
        return (dist >= 0) & (dist <= win) & (dist % dil == 0)

    mask = np.concatenate([visible(q - np.arange(P)[None, :] + d * P, g)
                           for g, n in ((0, 2), (1, 5), (2, PT)) for d in range(n - 1, -1, -1)], 1)
    t = np.arange(AW // HD * DS)[:, None] % DS
    cols = []
    for g, n in enumerate(PREV):
        r = np.arange(n)[None, :]
        if g == 2:
            r = r[:, (r[0] % 16) < DS]
        cols.append(visible(n + t - r, g))
    new = [visible(t - np.arange(DS)[None, :], g) for g in range(NG)]
    smask = np.concatenate([cols[0], *new, cols[1], cols[2]], 1)
    return {"c_ident": np.eye(P, dtype=np.float32),
            "c_cos": np.ascontiguousarray(cos.reshape(P, -1)), "c_sin": np.ascontiguousarray(sin.reshape(P, -1)),
            "c_mask_prompt": np.where(mask, 0.0, NEG).astype(np.float32),
            "c_mask_sample": np.where(smask, 0.0, NEG).astype(np.float32),
            "c_count": np.tile(np.arange(P, dtype=np.float32), (P, 1))}


def kernel(**inputs):
    import numpy as _np
    import concourse.bacc as _bacc
    from concourse import mybir as _mybir
    from concourse.bass_utils import run_bass_kernel_spmd as _run

    nc = _bacc.Bacc("TRN2", target_bir_lowering=False, num_devices=1)
    arrays, io = {}, {}
    for name in _INS:
        a = _np.ascontiguousarray(inputs[name])
        arrays[f"in_{name}_dram"] = a
        io[name] = nc.dram_tensor(f"in_{name}_dram", a.shape, _mybir.dt.from_np(a.dtype), kind="ExternalInput").ap()
    for name, a in shape_constants().items():
        arrays[f"in_{name}_dram"] = a
        io[name] = nc.dram_tensor(f"in_{name}_dram", a.shape, _mybir.dt.from_np(a.dtype), kind="ExternalInput").ap()
    for name, shape in _OUTS:
        io[name] = nc.dram_tensor(f"out_{name}_dram", shape, _mybir.dt.float32, kind="ExternalOutput").ap()
    program(nc, io)
    r = _run(nc, [arrays], core_ids=[0])
    return tuple(r.results[0][f"out_{name}_dram"] for name, _ in _OUTS)
```
